# Optimizing a Trainium2 kernel written in Bass

```python
import math
import jax
import jax.numpy as jnp
from jax import lax
import numpy as np
import jax, jax.numpy as jnp

D_MODEL = 1024
BATCH = 1
SEQ = 256
DEPTH = 2

N_A_LAYERS = DEPTH // 2
N_B_LAYERS = DEPTH - N_A_LAYERS

A_HEADS = 8
A_DK = 128
A_DV = 128
A_KEY_W = A_HEADS * A_DK
A_VAL_W = A_HEADS * A_DV
A_CONV_CH = 2 * A_KEY_W + A_VAL_W
A_IN_W = A_CONV_CH + A_VAL_W + 2 * A_HEADS
CONV_W = 4
CHUNK = 64

B_HEADS = 8
B_DH = 128
B_W = B_HEADS * B_DH
MOBA_BLOCK = 256
MOBA_TOPK = 3
Q_SUB = 32

N_BUCKETS = 32
MAX_DIST = 2048
EPS = 1e-6


def rms_norm(x, g):
    xf = x.astype(jnp.float32)
    y = xf * lax.rsqrt(jnp.mean(xf * xf, axis=-1, keepdims=True) + EPS)
    return (y * g.astype(jnp.float32)).astype(x.dtype)

def l2_normalize(t):
    tf = t.astype(jnp.float32)
    return tf * lax.rsqrt(jnp.sum(tf * tf, axis=-1, keepdims=True) + EPS)

def causal_conv_silu(u, w):
    c = u.shape[-1]
    up = jnp.pad(u, ((0, 0), (CONV_W - 1, 0), (0, 0)))
    out = lax.conv_general_dilated(up, w[:, None, :].astype(u.dtype), window_strides=(1,), padding="VALID", dimension_numbers=("NWC", "WIO", "NWC"), feature_group_count=c)
    return jax.nn.silu(out)

def gated_delta_rule(q, k, v, g, beta):
    bsz, s, h, dk = q.shape
    dv = v.shape[-1]
    n = s // CHUNK
    f32 = jnp.float32

    def to_chunks(t):
        t = t.astype(f32).reshape((bsz, n, CHUNK) + t.shape[2:])
        return jnp.moveaxis(t, 3, 1)

    q, k, v, g, beta = (to_chunks(t) for t in (q, k, v, g, beta))
    g = jnp.cumsum(g, axis=-1)
    idx = jnp.arange(CHUNK)
    tril = idx[:, None] >= idx[None, :]
    strict = idx[:, None] > idx[None, :]
    decay = jnp.exp(jnp.where(tril, g[..., :, None] - g[..., None, :], -jnp.inf))
    k_beta = k * beta[..., None]
    a_mat = jnp.where(strict, jnp.einsum("bhncd,bhnsd->bhncs", k_beta, k) * decay, 0.0)
    rhs = jnp.concatenate([v * beta[..., None], k_beta * jnp.exp(g)[..., None]], axis=-1)
    sol = lax.linalg.triangular_solve(a_mat + jnp.eye(CHUNK, dtype=f32), rhs, left_side=True, lower=True, unit_diagonal=True)
    u, w = sol[..., :dv], sol[..., dv:]
    qk_intra = jnp.where(tril, jnp.einsum("bhncd,bhnsd->bhncs", q, k) * decay, 0.0)
    q_dec = q * jnp.exp(g)[..., None]
    k_dec = k * jnp.exp(g[..., -1:] - g)[..., None]
    g_last = jnp.exp(g[..., -1])

    def step(state, xs):
        u_c, w_c, qd_c, qk_c, kd_c, gl_c = xs
        v_new = u_c - jnp.einsum("bhck,bhkv->bhcv", w_c, state)
        o = jnp.einsum("bhck,bhkv->bhcv", qd_c, state) + jnp.einsum("bhcs,bhsv->bhcv", qk_c, v_new)
        state = state * gl_c[..., None, None] + jnp.einsum("bhck,bhcv->bhkv", kd_c, v_new)
        return state, o

    xs = tuple(jnp.moveaxis(t, 2, 0) for t in (u, w, q_dec, qk_intra, k_dec, g_last))
    state0 = jnp.zeros((bsz, h, dk, dv), f32)
    _, o = lax.scan(step, state0, xs)
    return o.transpose(1, 0, 3, 2, 4).reshape(bsz, s, h, dv)

def gated_deltanet_mixer(hn, w_in, conv_w, a_log, dt_bias, out_norm_g, w_out):
    bsz, s, _ = hn.shape
    f32 = jnp.float32
    proj = hn @ w_in
    qkv = causal_conv_silu(proj[..., :A_CONV_CH], conv_w)
    z = proj[..., A_CONV_CH:A_CONV_CH + A_VAL_W]
    a = proj[..., A_CONV_CH + A_VAL_W:A_CONV_CH + A_VAL_W + A_HEADS]
    b = proj[..., A_CONV_CH + A_VAL_W + A_HEADS:]
    q = l2_normalize(qkv[..., :A_KEY_W].reshape(bsz, s, A_HEADS, A_DK)) * (A_DK ** -0.5)
    k = l2_normalize(qkv[..., A_KEY_W:2 * A_KEY_W].reshape(bsz, s, A_HEADS, A_DK))
    v = qkv[..., 2 * A_KEY_W:].reshape(bsz, s, A_HEADS, A_DV)
    g = -jnp.exp(a_log.astype(f32)) * jax.nn.softplus(a.astype(f32) + dt_bias.astype(f32))
    beta = jax.nn.sigmoid(b.astype(f32))
    o = gated_delta_rule(q, k, v, g, beta)
    o = rms_norm(o, out_norm_g) * jax.nn.silu(z.astype(f32)).reshape(bsz, s, A_HEADS, A_DV)
    return o.reshape(bsz, s, A_VAL_W).astype(hn.dtype) @ w_out

def t5_bucket(rel):
    n = jnp.maximum(rel, 0)
    max_exact = N_BUCKETS // 2
    nf = jnp.maximum(n, 1).astype(jnp.float32)
    large = max_exact + (jnp.log(nf / max_exact) / math.log(MAX_DIST / max_exact) * (N_BUCKETS - max_exact)).astype(jnp.int32)
    large = jnp.minimum(large, N_BUCKETS - 1)
    return jnp.where(n < max_exact, n, large)

def shared_kv(x, kv_norm_g, w_kv):
    bsz, s, _ = x.shape
    kv = rms_norm(x, kv_norm_g) @ w_kv
    n_blk = -(-s // MOBA_BLOCK)
    s_pad = n_blk * MOBA_BLOCK

    def blocks(t):
        t = jnp.pad(t.reshape(bsz, s, B_HEADS, B_DH), ((0, 0), (0, s_pad - s), (0, 0), (0, 0)))
        return t.reshape(bsz, n_blk, MOBA_BLOCK, B_HEADS, B_DH).transpose(0, 3, 1, 2, 4)

    kb = blocks(kv[..., :B_W])
    vb = blocks(kv[..., B_W:])
    k_mean = jnp.mean(kb.astype(jnp.float32), axis=3)
    return kb, vb, k_mean

def moba_attention(q, kb, vb, k_mean, rel_bias):
    bsz, s, h, d = q.shape
    n_blk = kb.shape[2]
    topk = min(MOBA_TOPK, n_blk)
    scale = d ** -0.5
    f32 = jnp.float32
    n_sub = s // Q_SUB
    q_sub = q.transpose(0, 2, 1, 3).reshape(bsz, h, n_sub, Q_SUB, d).transpose(2, 0, 1, 3, 4)
    bias_t = rel_bias.T.astype(f32)
    b_ix = jnp.arange(bsz)[:, None, None, None]
    h_ix = jnp.arange(h)[None, :, None, None]
    blk_ids = jnp.arange(n_blk)
    offs = jnp.arange(MOBA_BLOCK)

    def one_sub(args):
        qs, s_idx = args
        q_pos = s_idx * Q_SUB + jnp.arange(Q_SUB)
        cur = (s_idx * Q_SUB) // MOBA_BLOCK
        qf = qs.astype(f32)
        gate = jnp.einsum("bhqd,bhnd->bhqn", qf, k_mean)
        gate = jnp.where(blk_ids < cur, gate, -jnp.inf)
        _, sel = lax.top_k(gate, topk)
        sel_ok = jnp.arange(topk) < cur
        k_sel = kb[b_ix, h_ix, sel].astype(f32)
        v_sel = vb[b_ix, h_ix, sel].astype(f32)
        k_pos_sel = sel[..., None] * MOBA_BLOCK + offs
        s_sel = jnp.einsum("bhqd,bhqkjd->bhqkj", qf, k_sel) * scale
        s_sel = s_sel + bias_t[h_ix[..., None], t5_bucket(q_pos[:, None, None] - k_pos_sel)]
        s_sel = jnp.where(sel_ok[:, None], s_sel, -jnp.inf).reshape(bsz, h, Q_SUB, topk * MOBA_BLOCK)
        k_own = lax.dynamic_index_in_dim(kb, cur, axis=2, keepdims=False).astype(f32)
        v_own = lax.dynamic_index_in_dim(vb, cur, axis=2, keepdims=False).astype(f32)
        rel_own = q_pos[:, None] - (cur * MOBA_BLOCK + offs)[None, :]
        s_own = jnp.einsum("bhqd,bhjd->bhqj", qf, k_own) * scale + bias_t[:, t5_bucket(rel_own)]
        s_own = jnp.where(rel_own >= 0, s_own, -jnp.inf)
        p = jax.nn.softmax(jnp.concatenate([s_sel, s_own], axis=-1), axis=-1)
        p_sel = p[..., :topk * MOBA_BLOCK].reshape(bsz, h, Q_SUB, topk, MOBA_BLOCK)
        p_own = p[..., topk * MOBA_BLOCK:]
        o = jnp.einsum("bhqkj,bhqkjd->bhqd", p_sel, v_sel) + jnp.einsum("bhqj,bhjd->bhqd", p_own, v_own)
        return o.astype(qs.dtype)

    o = lax.map(one_sub, (q_sub, jnp.arange(n_sub)))
    return o.transpose(1, 0, 3, 2, 4).reshape(bsz, s, h * d)

def moba_mixer(hn, w_in, w_out, kb, vb, k_mean, rel_bias):
    bsz, s, _ = hn.shape
    proj = hn @ w_in
    q = proj[..., :B_W].reshape(bsz, s, B_HEADS, B_DH)
    z = proj[..., B_W:]
    o = moba_attention(q, kb, vb, k_mean, rel_bias)
    return (o * jax.nn.silu(z)).astype(hn.dtype) @ w_out

def first_inputs(seed: int = 0) -> dict:
    key = jax.random.key(seed)
    ks = jax.random.split(key, 16)
    f32 = jnp.float32
    na, nb = N_A_LAYERS, N_B_LAYERS

    def gain(k, shape):
        return 1.0 + 0.01 * jax.random.normal(k, shape, f32)

    x = jax.random.normal(ks[0], (BATCH, SEQ, D_MODEL), f32)
    a_norm_g = gain(ks[1], (na, D_MODEL))
    a_w_in = jax.random.normal(ks[2], (na, D_MODEL, A_IN_W), f32) * D_MODEL ** -0.5
    a_conv_w = jax.random.normal(ks[3], (na, CONV_W, A_CONV_CH), f32) * CONV_W ** -0.5
    a_log = jnp.log(jax.random.uniform(ks[4], (na, A_HEADS), f32, 1.0, 16.0))
    dt = jnp.exp(jax.random.uniform(ks[5], (na, A_HEADS), f32, math.log(1e-3), math.log(1e-1)))
    a_dt_bias = dt + jnp.log(-jnp.expm1(-dt))
    a_out_norm_g = gain(ks[6], (na, A_DV))
    a_w_out = jax.random.normal(ks[7], (na, A_VAL_W, D_MODEL), f32) * A_VAL_W ** -0.5
    kv_norm_g = gain(ks[8], (D_MODEL,))
    w_kv = jax.random.normal(ks[9], (D_MODEL, 2 * B_W), f32) * D_MODEL ** -0.5
    b_norm_g = gain(ks[10], (nb, D_MODEL))
    b_w_in = jax.random.normal(ks[11], (nb, D_MODEL, 2 * B_W), f32) * D_MODEL ** -0.5
    b_w_out = jax.random.normal(ks[12], (nb, B_W, D_MODEL), f32) * B_W ** -0.5
    rel_bias = 0.2 * jax.random.normal(ks[13], (N_BUCKETS, B_HEADS), f32)
    final_norm_g = gain(ks[14], (D_MODEL,))
    return {"x": x, "a_norm_g": a_norm_g, "a_w_in": a_w_in, "a_conv_w": a_conv_w, "a_log": a_log, "a_dt_bias": a_dt_bias, "a_out_norm_g": a_out_norm_g, "a_w_out": a_w_out, "kv_norm_g": kv_norm_g, "w_kv": w_kv, "b_norm_g": b_norm_g, "b_w_in": b_w_in, "b_w_out": b_w_out, "rel_bias": rel_bias, "final_norm_g": final_norm_g}

def first_block(x, a_norm_g, a_w_in, a_conv_w, a_log, a_dt_bias, a_out_norm_g, a_w_out, kv_norm_g, w_kv, b_norm_g, b_w_in, b_w_out, rel_bias, final_norm_g):
    shared = None
    for layer in range(DEPTH):
        if layer < N_A_LAYERS:
            i = layer
            x = x + gated_deltanet_mixer(rms_norm(x, a_norm_g[i]), a_w_in[i], a_conv_w[i], a_log[i], a_dt_bias[i], a_out_norm_g[i], a_w_out[i])
        else:
            if shared is None:
                shared = shared_kv(x, kv_norm_g, w_kv)
            j = layer - N_A_LAYERS
            kb, vb, k_mean = shared
            x = x + moba_mixer(rms_norm(x, b_norm_g[j]), b_w_in[j], b_w_out[j], kb, vb, k_mean, rel_bias)
    return rms_norm(x, final_norm_g)


N_MIXERS = 2

RET_HEADS = 4
RET_QK_DIM = D_MODEL // RET_HEADS
RET_V_DIM = 2 * D_MODEL // RET_HEADS
RET_QK_WIDTH = RET_HEADS * RET_QK_DIM
RET_WIDTH = RET_HEADS * RET_V_DIM
ROPE_BASE = 10000.0

ATT_HEADS = 16
ATT_HEAD_DIM = 2 * D_MODEL // ATT_HEADS
ATT_WIDTH = ATT_HEADS * ATT_HEAD_DIM
LEFT_CHUNKS = 8
BAND = (LEFT_CHUNKS + 1) * CHUNK
MAX_REL = 2 * CHUNK

N_RET_LAYERS = (DEPTH + 1) // 2
N_ATT_LAYERS = DEPTH // 2


def rms_norm_f32(t, gain):
    t32 = t.astype(jnp.float32)
    return t32 * lax.rsqrt(jnp.mean(t32 * t32, axis=-1, keepdims=True) + EPS) * gain.astype(jnp.float32)

def apply_rope(t, cos, sin):
    t1, t2 = jnp.split(t, 2, axis=-1)
    return jnp.concatenate([t1 * cos - t2 * sin, t1 * sin + t2 * cos], axis=-1)

def retention_mixer(h, positions, w_in, gn_g, w_out):
    B, S, _ = h.shape
    nc = S // CHUNK
    proj = h @ w_in
    q, k, v, g = jnp.split(proj, [RET_QK_WIDTH, 2 * RET_QK_WIDTH, 2 * RET_QK_WIDTH + RET_WIDTH], axis=-1)
    q = q.reshape(B, S, RET_HEADS, RET_QK_DIM).astype(jnp.float32)
    k = k.reshape(B, S, RET_HEADS, RET_QK_DIM).astype(jnp.float32)
    v = v.reshape(B, S, RET_HEADS, RET_V_DIM).astype(jnp.float32)

    inv_freq = 1.0 / (ROPE_BASE ** (jnp.arange(0, RET_QK_DIM, 2, dtype=jnp.float32) / RET_QK_DIM))
    ang = positions.astype(jnp.float32)[..., None] * inv_freq
    cos, sin = jnp.cos(ang)[:, :, None, :], jnp.sin(ang)[:, :, None, :]
    q = apply_rope(q, cos, sin)
    k = apply_rope(k, cos, sin) * (RET_QK_DIM ** -0.5)

    def to_chunks(t):
        return t.reshape(B, nc, CHUNK, RET_HEADS, t.shape[-1]).transpose(0, 3, 1, 2, 4)

    qc, kc, vc = to_chunks(q), to_chunks(k), to_chunks(v)

    log_gamma = jnp.log(1.0 - 2.0 ** (-5.0 - jnp.arange(RET_HEADS, dtype=jnp.float32)))
    idx = jnp.arange(CHUNK, dtype=jnp.float32)
    intra_decay = jnp.exp(log_gamma[:, None, None] * jnp.abs(idx[:, None] - idx[None, :]))
    q_decay = jnp.exp(log_gamma[:, None] * (idx + 1.0))
    k_decay = jnp.exp(log_gamma[:, None] * (CHUNK - 1.0 - idx))
    chunk_decay = jnp.exp(log_gamma * CHUNK)

    scores = jnp.einsum('bhncd,bhnkd->bhnck', qc, kc) * intra_decay[:, None]
    o_intra = jnp.einsum('bhnck,bhnke->bhnce', scores, vc)

    def step(state, xs):
        q_j, k_j, v_j = xs
        o_j = jnp.einsum('bhcd,bhde->bhce', q_j * q_decay[:, :, None], state)
        state = chunk_decay[:, None, None] * state + jnp.einsum(
            'bhcd,bhce->bhde', k_j * k_decay[:, :, None], v_j)
        return state, o_j

    xs = (qc.transpose(2, 0, 1, 3, 4), kc.transpose(2, 0, 1, 3, 4), vc.transpose(2, 0, 1, 3, 4))
    state0 = jnp.zeros((B, RET_HEADS, RET_QK_DIM, RET_V_DIM), jnp.float32)
    _, o_inter = lax.scan(step, state0, xs)

    o = o_intra + o_inter.transpose(1, 2, 0, 3, 4)
    o = o.transpose(0, 2, 3, 1, 4).reshape(B, S, RET_HEADS, RET_V_DIM)
    o = rms_norm_f32(o, gn_g.reshape(RET_HEADS, RET_V_DIM))
    o = o.reshape(B, S, RET_WIDTH) * jax.nn.silu(g.astype(jnp.float32))
    return o.astype(h.dtype) @ w_out

def chunked_attention_mixer(h, w_in, q_g, k_g, rel_table, w_out):
    B, S, _ = h.shape
    nc = S // CHUNK
    proj = h @ w_in
    q, k, v, g = jnp.split(proj, 4, axis=-1)
    q = rms_norm_f32(q.reshape(B, S, ATT_HEADS, ATT_HEAD_DIM), q_g)
    k = rms_norm_f32(k.reshape(B, S, ATT_HEADS, ATT_HEAD_DIM), k_g)
    v = v.reshape(B, S, ATT_HEADS, ATT_HEAD_DIM).astype(jnp.float32)

    pad = LEFT_CHUNKS * CHUNK
    k_pad = jnp.pad(k, ((0, 0), (pad, 0), (0, 0), (0, 0)))
    v_pad = jnp.pad(v, ((0, 0), (pad, 0), (0, 0), (0, 0)))

    qi = jnp.arange(CHUNK)
    kb = jnp.arange(BAND)
    rel = qi[:, None] + pad - kb[None, :]
    bias = rel_table.astype(jnp.float32)[:, jnp.clip(rel, -MAX_REL, MAX_REL) + MAX_REL]
    scale = ATT_HEAD_DIM ** -0.5

    q_chunks = q.reshape(B, nc, CHUNK, ATT_HEADS, ATT_HEAD_DIM).transpose(1, 0, 2, 3, 4)

    def one_chunk(args):
        j, q_j = args
        k_j = lax.dynamic_slice_in_dim(k_pad, j * CHUNK, BAND, axis=1)
        v_j = lax.dynamic_slice_in_dim(v_pad, j * CHUNK, BAND, axis=1)
        s = jnp.einsum('bqhd,bkhd->bhqk', q_j, k_j) * scale + bias
        valid = kb >= (LEFT_CHUNKS - j) * CHUNK
        s = jnp.where(valid, s, jnp.float32(-1e30))
        p = jax.nn.softmax(s, axis=-1)
        return jnp.einsum('bhqk,bkhd->bqhd', p, v_j)

    o = lax.map(one_chunk, (jnp.arange(nc), q_chunks))
    o = o.transpose(1, 0, 2, 3, 4).reshape(B, S, ATT_WIDTH)
    o = o * jax.nn.silu(g.astype(jnp.float32))
    return o.astype(h.dtype) @ w_out

def second_inputs(seed: int = 0) -> dict:
    key = jax.random.key(seed)
    ks = jax.random.split(key, 16)
    D = D_MODEL
    x = jax.random.normal(ks[0], (BATCH, SEQ, D), jnp.float32)
    c = jax.random.normal(ks[1], (BATCH, D), jnp.float32)
    offsets = jax.random.randint(ks[2], (BATCH, 1), 0, 4096, dtype=jnp.int32)
    positions = offsets + jnp.arange(SEQ, dtype=jnp.int32)[None, :]
    norm_g = 1.0 + 0.1 * jax.random.normal(ks[3], (DEPTH, D), jnp.float32)
    ada_w = jax.random.normal(ks[4], (DEPTH, D, 3 * D), jnp.float32) * D ** -0.5
    ada_b = 0.02 * jax.random.normal(ks[5], (DEPTH, 3 * D), jnp.float32)
    ret_w_in = jax.random.normal(ks[6], (N_RET_LAYERS, D, 2 * RET_QK_WIDTH + 2 * RET_WIDTH), jnp.float32) * D ** -0.5
    ret_gn_g = 1.0 + 0.1 * jax.random.normal(ks[7], (N_RET_LAYERS, RET_WIDTH), jnp.float32)
    ret_w_out = jax.random.normal(ks[8], (N_RET_LAYERS, RET_WIDTH, D), jnp.float32) * RET_WIDTH ** -0.5
    att_w_in = jax.random.normal(ks[9], (N_ATT_LAYERS, D, 4 * ATT_WIDTH), jnp.float32) * D ** -0.5
    att_q_g = 1.0 + 0.1 * jax.random.normal(ks[10], (N_ATT_LAYERS, ATT_HEAD_DIM), jnp.float32)
    att_k_g = 1.0 + 0.1 * jax.random.normal(ks[11], (N_ATT_LAYERS, ATT_HEAD_DIM), jnp.float32)
    att_rel_bias = 0.5 * jax.random.normal(ks[12], (N_ATT_LAYERS, ATT_HEADS, 2 * MAX_REL + 1), jnp.float32)
    att_w_out = jax.random.normal(ks[13], (N_ATT_LAYERS, ATT_WIDTH, D), jnp.float32) * ATT_WIDTH ** -0.5
    return {"x": x, "c": c, "positions": positions, "norm_g": norm_g, "ada_w": ada_w,
            "ada_b": ada_b, "ret_w_in": ret_w_in, "ret_gn_g": ret_gn_g, "ret_w_out": ret_w_out,
            "att_w_in": att_w_in, "att_q_g": att_q_g, "att_k_g": att_k_g,
            "att_rel_bias": att_rel_bias, "att_w_out": att_w_out}

def second_block(x, c, positions, norm_g, ada_w, ada_b, ret_w_in, ret_gn_g, ret_w_out,
              att_w_in, att_q_g, att_k_g, att_rel_bias, att_w_out):
    cond = jax.nn.silu(c.astype(jnp.float32))
    for i in range(DEPTH):
        mod = cond @ ada_w[i].astype(jnp.float32) + ada_b[i].astype(jnp.float32)
        shift, scale, gate = jnp.split(mod[:, None, :], 3, axis=-1)
        h = (rms_norm_f32(x, norm_g[i]) * (1.0 + scale) + shift).astype(x.dtype)
        j = i // N_MIXERS
        if i % N_MIXERS == 0:
            out = retention_mixer(h, positions, ret_w_in[j], ret_gn_g[j], ret_w_out[j])
        else:
            out = chunked_attention_mixer(h, att_w_in[j], att_q_g[j], att_k_g[j],
                                          att_rel_bias[j], att_w_out[j])
        x = x + (gate * out.astype(jnp.float32)).astype(x.dtype)
    return x


def setup_inputs(seed=0):
    out = dict(first_inputs(seed))
    for name, value in second_inputs(seed + 1).items():
        if name != "x":
            out[name + "_2"] = value
    return out


def reference(
    x, a_norm_g, a_w_in, a_conv_w, a_log, a_dt_bias, a_out_norm_g, a_w_out, kv_norm_g, w_kv,
    b_norm_g, b_w_in, b_w_out, rel_bias, final_norm_g, c_2, positions_2, norm_g_2, ada_w_2,
    ada_b_2, ret_w_in_2, ret_gn_g_2, ret_w_out_2, att_w_in_2, att_q_g_2, att_k_g_2,
    att_rel_bias_2, att_w_out_2,
):
    x = first_block(
        x, a_norm_g, a_w_in, a_conv_w, a_log, a_dt_bias, a_out_norm_g, a_w_out, kv_norm_g, w_kv,
        b_norm_g, b_w_in, b_w_out, rel_bias, final_norm_g,
    )
    return second_block(
        x, c_2, positions_2, norm_g_2, ada_w_2, ada_b_2, ret_w_in_2, ret_gn_g_2, ret_w_out_2,
        att_w_in_2, att_q_g_2, att_k_g_2, att_rel_bias_2, att_w_out_2,
    )


_drawn_inputs = setup_inputs


def setup_inputs(seed=0):
    import zlib

    import numpy as np

    out = dict(_drawn_inputs(seed))
    spreads = {}
    factors = {'a_norm_g': 4.999,
     'a_out_norm_g': 8.0,
     'kv_norm_g': 8.0,
     'b_norm_g': 8.0,
     'rel_bias': 2.736,
     'final_norm_g': 4.723,
     'att_q_g_2': 7.877,
     'att_k_g_2': 7.725}
    for name, (base, spread) in spreads.items():
        noise = np.random.default_rng([zlib.crc32(name.encode()), seed]).standard_normal(out[name].shape)
        drawn = base * np.exp(spread * noise) if base else spread * noise
        out[name] = jnp.asarray(drawn.astype(out[name].dtype))
    for name, factor in factors.items():
        out[name] = (out[name] * factor).astype(out[name].dtype)
    return out
```

```python
import numpy as np
import concourse.bass as bass
from concourse import mybir
from contextlib import ExitStack

P = 128
S = 256
D = 1024
KT = D // P
HEADS = 8
DH = 128
EPS = 1e-6
F32 = mybir.dt.float32
F32R = mybir.dt.float32r
I32 = mybir.dt.int32
U8 = mybir.dt.uint8
ALU = mybir.AluOpType
ACT = mybir.ActivationFunctionType
AX = mybir.AxisListType
NEG = -1e30

COLS = {}
_at = 0
for _name, _n in (("a_norm", 8), ("kv_norm", 8), ("b_norm", 8), ("final_norm", 8), ("norm2", 16), ("ret_gn", 16),
                  ("att_q", 1), ("att_k", 1), ("a_out", 1), ("conv", 96), ("cond", 8), ("ada_b", 48), ("rows", 2),
                  ("inv_freq", 1)):
    COLS[_name] = _at
    _at += _n
N_COLS = _at
C_IDENT, C_CAUSAL, C_STRICT, C_ONEHOT, N_CONST = 0, 128, 256, 384, 640
LEVELS = 7
N_CHUNKS = 112
RAW = 3
UNITS = 4
ADA_UNITS = 48

JOB_OUT_A, JOB_B, JOB_OUT_B, JOB_C, JOB_OUT_C, JOB_D, JOB_OUT_D, N_JOBS = 16, 20, 36, 40, 64, 68, 100, 104


def chunks_of(job):
    if job < JOB_OUT_C:
        return [job]
    if job < JOB_D:
        return [JOB_OUT_C + 2 * (job - JOB_OUT_C) + h for h in range(2)]
    if job < JOB_OUT_D:
        return [job + 4]
    return [JOB_OUT_D + 4 + 2 * (job - JOB_OUT_D) + h for h in range(2)]


def two_blocks(nc, x_in, wts, ada_w, cols_in, const_in, lmask_in, w_ab, rel_b, rel_d, dtab, pos, out,
               scr_b, scr_d):
    ctx = ExitStack()
    with ctx:
        def sb(name, shape, dt=F32):
            return ctx.enter_context(nc.sbuf_tensor(name, shape, dt))

        def sem(name):
            return ctx.enter_context(nc.semaphore(name))

        raw = sb("raw", [P, RAW, KT, 256])
        whi = sb("whi", [P, UNITS, 4, 256], F32R)
        wlo = sb("wlo", [P, UNITS, 4, 256], F32R)
        hhi = sb("hhi", [P, KT, S], F32R)
        hlo = sb("hlo", [P, KT, S], F32R)
        ohi = sb("ohi", [P, 16, S], F32R)
        olo = sb("olo", [P, 16, S], F32R)
        x = sb("x", [P, KT, S])
        ring = sb("ada_ring", [P, 2, KT, 128])
        cols = sb("columns", [P, N_COLS])
        cst = sb("cst", [P, N_CONST])
        ones = sb("ones", [P, P])
        epsc = sb("epsc", [P, 2])
        mod = sb("mod", [P, 48])
        gsc = sb("gsc", [P, 16])
        sil = sb("sil", [P, KT])
        ar = sb("arena", [P, 18432])

        ident = cst[:, C_IDENT:C_IDENT + P]
        causal = cst[:, C_CAUSAL:C_CAUSAL + P]
        strict = cst[:, C_STRICT:C_STRICT + P]
        onehot = cst[0:32, C_ONEHOT:C_ONEHOT + S]

        def col(name, k=0):
            return cols[:, COLS[name] + k:COLS[name] + k + 1]

        def A(at, *shape, parts=P):
            n = int(np.prod(shape))
            v = ar[0:parts, at:at + n]
            if len(shape) == 2:
                v = v.rearrange("p (a b) -> p a b", a=shape[0])
            if len(shape) == 3:
                v = v.rearrange("p (a b c) -> p a b c", a=shape[0], b=shape[1])
            return v

        qh, kh, zt = A(0, 8, S), A(2048, 8, S), A(4096, 8, S)
        vb = A(6144, 16, P)
        kdec, kbe = A(8192, 8, P), A(9216, 8, P)
        qkd = A(10240, 16, P)
        nt = A(12288, 16, P)
        tt = A(14336, 16, P)
        uu = A(16384, 16, P)
        hf_a, xsq_a = A(10240, 8, S), A(12288, 8, S)
        pre = A(14336, 6, 259)
        sq_a, rs_a = A(16384, 4, S), A(13312, 4, S)
        vsil = A(17920, 2, S)
        raw_a = A(12288, 4, S)
        st1, vn0, vn1, wt_ = A(12288, 8, P), A(13312, 8, P), A(14336, 8, P), A(2048, 8, P)
        osq, ors, oof = A(15360, 4, S), A(3072, 4, S), A(8192, 2, S)
        pp = ring[:, 0:1, :, :].rearrange("p a b c -> p (a b c)")[:, 0:1024].rearrange("p (a b) -> p a b", a=4)
        ee = ring[:, 1:2, :, :].rearrange("p a b c -> p (a b c)")[:, 0:512].rearrange("p (a b) -> p a b", a=4)
        ke = ring[:, 1:2, :, :].rearrange("p a b c -> p (a b c)")[:, 512:1024].rearrange("p (a b) -> p a b", a=4)
        r16 = sb("r16", [16, 6, S])
        lmask = sb("lmask", [P, LEVELS, 256], U8)
        mask_in = A(9216, LEVELS * 64).bitcast(I32)
        hc = sb("hc", [P, 5, 16])

        bias_at = 0
        hf, xsq = A(6144, 8, S), A(8192, 8, S)
        qraw, kraw = A(10240, 2, S), A(10752, 2, S)
        qn, kn = A(11264, 2, S), A(11776, 2, S)
        sqb, rsb = A(12288, 4, S), A(13312, 4, S)
        zs = A(14336, 4, S)
        vs = A(15360, 2, 512)
        ts = A(16384, 2, 384)
        pt = A(17152, 2, 384)
        of = A(8192, 2, S)
        sm = A(17920, 4, 4)
        cost, sint = A(0, S), A(256, S)
        dmat = A(512, 4, 384)
        rt1, rt2 = A(16384, 2, S), A(16896, 2, S)
        sd = A(17408, 384)
        posi = A(2048, S).bitcast(I32)
        ang = A(2304, S)
        tr1, tr2 = A(2560, S), A(2816, S)
        sq4 = A(2048, 4, S)
        zs_c = A(6144, 8, S)
        fb = sb("fb", [16, 512])
        rcol = sb("rcol", [16, 1])

        ps = [ctx.enter_context(nc.psum_tensor(f"ps{i}", [P, 512], F32)) for i in range(8)]
        pj = [ps[0], ps[1]]
        ssb = ps[2]

        def v2(b, w=S):
            return b[:, :].rearrange("p (a b) -> p a b", b=w)

        x_in_sem = sem("x_in")
        cols_in_sem = sem("cols_in")
        const_in_sem = sem("const_in")
        ab_in_sem = sem("ab_in")
        rel_in_sem = sem("rel_in")
        rel_d_in_sem = sem("rel_d_in")
        lmask_in_sem = sem("lmask_in")
        pos_in_sem = sem("pos_in")
        dtab_in_sem = sem("dtab_in")
        ones_ok_sem = sem("ones_ok")
        w_units_sem = sem("w_units")
        hi_ok_sem = sem("hi_ok")
        lo_ok_sem = sem("lo_ok")
        sq_ok_sem = sem("sq_ok")
        ss_ok_sem = sem("ss_ok")
        ss_read_sem = sem("ss_read")
        rs_ok_sem = sem("rs_ok")
        hf_ok_sem = sem("hf_ok")
        hh_ok_sem = sem("hh_ok")
        h_ok_sem = sem("h_ok")
        dve_own_sem = sem("dve_own")
        ab_ok_sem = sem("ab_ok")
        rows_ok_sem = sem("rows_ok")
        scan_ok_sem = sem("scan_ok")
        rowsT_ok_sem = sem("rowsT_ok")
        bcol_ok_sem = sem("bcol_ok")
        conv_ok_sem = sem("conv_ok")
        qk_raw_sem = sem("qk_raw")
        qk_sq_sem = sem("qk_sq")
        qk_ok_sem = sem("qk_ok")
        vsil_ok_sem = sem("vsil_ok")
        vT_ok_sem = sem("vT_ok")
        vb_ok_sem = sem("vb_ok")
        delta_in_sem = sem("delta_in")
        gl_ok_sem = sem("gl_ok")
        e_pre_sem = sem("e_pre")
        e_ok_sem = sem("e_ok")
        nt_ok_sem = sem("nt_ok")
        kT_ok_sem = sem("kT_ok")
        kcol_ok_sem = sem("kcol_ok")
        p_ok_sem = sem("p_ok")
        pe_v_sem = sem("pe_v")
        tp_ok_sem = sem("tp_ok")
        t_ok_sem = sem("t_ok")
        ut_ok_sem = sem("ut_ok")
        u_ok_sem = sem("u_ok")
        un_ok_sem = sem("un_ok")
        vn_ok_sem = sem("vn_ok")
        st_ok_sem = sem("st_ok")
        stv_sem = sem("stv")
        wt_ok_sem = sem("wt_ok")
        wv_sem = sem("wv")
        vn1_ok_sem = sem("vn1_ok")
        vn1v_sem = sem("vn1v")
        o_ok_sem = sem("o_ok")
        o_sq_sem = sem("o_sq")
        egb_sem = sem("egb")
        o_split_sem = sem("o_split")
        sil_ok_sem = sem("sil_ok")
        ada_used_sem = sem("ada_used")
        mod_ok_sem = sem("mod_ok")
        sc_ok_sem = sem("sc_ok")
        m_ok_sem = sem("m_ok")
        mask_ok_sem = sem("mask_ok")
        bias_ps_sem = sem("bias_ps")
        bias_sb_sem = sem("bias_sb")
        scr_out_sem = sem("scr_out")
        bias_ok_sem = sem("bias_ok")
        s_ok_sem = sem("s_ok")
        t_soft_sem = sem("t_soft")
        e_soft_sem = sem("e_soft")
        p_soft_sem = sem("p_soft")
        pT_ok_sem = sem("pT_ok")
        pT_v_sem = sem("pT_v")
        fin_rope_sem = sem("fin_rope")
        rope_ok_sem = sem("rope_ok")
        sd_ok_sem = sem("sd_ok")
        out_ok_sem = sem("out_ok")
        xn_ok_sem = sem("xn_ok")
        ce_sem = sem("ce")
        boot_sem = sem("boot")
        rowsv_sem = sem("rowsv")
        raw_in = [sem(f"raw_in{i}") for i in range(RAW)]
        ada_in = [sem(f"ada_in{i}") for i in range(2)]
        bank_free = [sem(f"bank_free{i}") for i in range(2)]
        block = ctx.enter_context(nc.Block())

        @block.sync
        def _(sp):
            sp.dma_start(x[:, 0:4, :], x_in[:, 0:4, :]).then_inc(x_in_sem, 16)
            sp.dma_start(x[:, 4:8, :], x_in[:, 4:8, :]).then_inc(x_in_sem, 16)
            sp.dma_start(cols[:, :], cols_in).then_inc(cols_in_sem, 16)
            for c in range(N_CHUNKS):
                if c >= RAW:
                    sp.wait_ge(lo_ok_sem, max(2 * (c - RAW) + 2, 0))
                sp.dma_start(raw[:, c % RAW, :, :].rearrange("p a b -> p (a b)"), wts[c]).then_inc(raw_in[c % RAW], 16)
                if c == 0:
                    sp.dma_start(cst[:, :], const_in).then_inc(const_in_sem, 16)
                    sp.dma_start(A(6144, 8, 16), w_ab).then_inc(ab_in_sem, 16)
                    sp.dma_start(mask_in, lmask_in).then_inc(lmask_in_sem, 16)
                    sp.dma_start(A(8192, 8, parts=32), rel_b).then_inc(rel_in_sem, 16)
                if c == JOB_C:
                    sp.wait_ge(t_soft_sem, 8)
                    sp.dma_start(posi[:, :], pos.partition_broadcast(P)).then_inc(pos_in_sem, 16)
                    sp.dma_start(dmat[:, :, :], dtab).then_inc(dtab_in_sem, 16)
            for b in range(2):
                sp.wait_ge(bank_free[b], N_JOBS // 2)
            sp.dma_start(out, x[:, :, :]).then_inc(out_ok_sem, 16)
            sp.wait_ge(out_ok_sem, 16)

        @block.gpsimd
        def _(pool):
            pool.memset(ones[:, :], 1.0).then_inc(ones_ok_sem, 1)
            pool.memset(epsc[:, 0:1], EPS).then_inc(ones_ok_sem, 1)
            pool.memset(epsc[:, 1:2], 1.0).then_inc(ones_ok_sem, 1)
            pool.memset(pre[:, :, 0:3], 0.0).then_inc(ones_ok_sem, 1)
            pool.memset(fb[0:8, 256:512], NEG).then_inc(ones_ok_sem, 1)
            pool.memset(r16[:, 5, :], 1.0).then_inc(ones_ok_sem, 1)
            pool.wait_ge(lmask_in_sem, 16)
            for lv in range(LEVELS):
                pool.tensor_copy(lmask[:, lv, :].rearrange("p (a b) -> p a b", a=4),
                                 mask_in[:, 64 * lv:64 * lv + 64].unsqueeze(1).to_broadcast([P, 4, 64])).then_inc(mask_ok_sem, 1)
            for u in range(24):
                pool.wait_ge(ada_used_sem, max(u - 1, 0))
                pool.dma_start(ring[:, u % 2, :, :].rearrange("p a b -> p (a b)"), ada_w[u]).then_inc(ada_in[u % 2], 16)
            pool.wait_ge(bias_sb_sem, 1)
            pool.dma_start(scr_b.rearrange("p h t -> h p t"), fb[0:8, :].unsqueeze(1).to_broadcast([8, P, 512])).then_inc(scr_out_sem, 16)
            pool.wait_ge(scr_out_sem, 16)
            pool.wait_ge(o_split_sem, 4)
            bias_b = A(bias_at, 8, 384)
            pool.dma_start(bias_b[:, :, 0:256], bass.AP(scr_b.tensor, 127, [[8 * 512 - 1, P], [512, 8], [1, 256]])).then_inc(bias_ok_sem, 16)
            pool.dma_start(bias_b[:, :, 256:384], bass.AP(scr_b.tensor, 255, [[8 * 512 - 1, P], [512, 8], [1, 128]])).then_inc(bias_ok_sem, 16)
            for u in range(24, ADA_UNITS):
                pool.wait_ge(ada_used_sem, max(u - 1, 0))
                pool.dma_start(ring[:, u % 2, :, :].rearrange("p a b -> p (a b)"), ada_w[u]).then_inc(ada_in[u % 2], 16)
            pool.wait_ge(bias_sb_sem, 1)
            pool.dma_start(fb[:, 127:384], rel_d).then_inc(rel_d_in_sem, 16)
            pool.wait_ge(rel_d_in_sem, 16)
            pool.tensor_scalar(fb[:, 0:127], fb[:, 127:254], 0.0, fb[:, 127:128], ALU.mult, ALU.add).then_inc(boot_sem, 1)
            pool.tensor_scalar(fb[:, 384:512], fb[:, 255:383], 0.0, fb[:, 383:384], ALU.mult, ALU.add).then_inc(boot_sem, 1)
            pool.wait_ge(boot_sem, 2)
            pool.dma_start(scr_d.rearrange("p h t -> h p t"), fb[:, :].unsqueeze(1).to_broadcast([16, P, 512])).then_inc(scr_out_sem, 16)
            pool.wait_ge(scr_out_sem, 32)
            pool.wait_ge(o_split_sem, 12)
            bias_d = A(bias_at, 16, 384)
            for h0 in range(0, 16, 8):
                pool.dma_start(bias_d[:, h0:h0 + 8, 0:256], bass.AP(scr_d.tensor, 127 + 512 * h0, [[16 * 512 - 1, P], [512, 8], [1, 256]])).then_inc(bias_ok_sem, 16)
                pool.dma_start(bias_d[:, h0:h0 + 8, 256:384], bass.AP(scr_d.tensor, 255 + 512 * h0, [[16 * 512 - 1, P], [512, 8], [1, 128]])).then_inc(bias_ok_sem, 16)
            pool.wait_ge(bias_ok_sem, 32 + 64)
            pool.memset(bias_d[0:64, :, 192:256], NEG).then_inc(boot_sem, 1)
            pool.memset(bias_d[0:64, :, 320:384], NEG).then_inc(boot_sem, 1)

        @block.tensor
        def _(pe):
            own_ss = [0]

            def mm(o, l, r, start, stop, skip=True):
                return pe.matmul(o, l, r, start=start, stop=stop, skip_group_check=skip)

            def job(J, form, hi, lo, ready=None):
                bank = v2(pj[J % 2])
                pe.wait_ge(bank_free[J % 2], J // 2)
                cs = chunks_of(J)
                for n, c in enumerate(cs):
                    for half in range(2):
                        unit = 2 * c + half
                        pe.wait_ge(lo_ok_sem, unit + 1)
                        for kk in range(4):
                            k = 4 * half + kk
                            kx = 8 * n + k
                            if ready is not None and k % 2 == 0 and n == 0:
                                pe.wait_ge(h_ok_sem, ready + k // 2 + 1)
                            for t in range(2):
                                w = slice(t * P, t * P + P)
                                for a, (ws, hs) in enumerate(((whi, hi), (whi, lo), (wlo, hi))):
                                    first = n == 0 and k == 0 and t == 0 and a == 0
                                    last = n == len(cs) - 1 and k == KT - 1 and a == 2
                                    if form == "T":
                                        m = mm(bank[:, t, :], ws[:, unit % UNITS, kk, w], hs[:, kx, :], first, last)
                                    else:
                                        m = mm(bank[:, t, :], hs[:, kx, w], ws[:, unit % UNITS, kk, :], first, last)
                        m.then_inc(w_units_sem, 1)

            def sums(src, n, width, cnt_sem, cnt):
                pe.wait_ge(ss_read_sem, own_ss[0])
                for t in range(n):
                    if cnt_sem is not None:
                        pe.wait_ge(cnt_sem, cnt(t))
                    m = mm(ssb[:, 0:width], ones[:, :], src(t), t == 0, t == n - 1)
                m.then_inc(ss_ok_sem, 1)
                own_ss[0] += 1

            def ada(u):
                pe.wait_ge(ada_in[u % 2], 16 * (u // 2 + 1))
                pe.wait_ge(sil_ok_sem, 1)
                if u % 6 == 0:
                    pe.wait_ge(mod_ok_sem, u // 6)
                for k in range(KT):
                    m = mm(ps[7][:, u % 6:u % 6 + 1], ring[:, u % 2, k, :], sil[:, k:k + 1], k == 0, k == KT - 1)
                m.then_inc(ada_used_sem, 1)

            pe.wait_ge(ones_ok_sem, 6)
            sums(lambda t: xsq_a[:, t, :], 8, S, sq_ok_sem, lambda t: t // 2 + 1)
            pe.wait_ge(const_in_sem, 16)

            def turn_values(i):
                pe.wait_ge(vsil_ok_sem, i + 1)
                pe.wait_ge(vb_ok_sem, i)
                for n in range(4):
                    m = pe.transpose(ps[3][:, n * P:n * P + P], vsil[:, n // 2, (n % 2) * P:(n % 2) * P + P], ident)
                m.then_inc(vT_ok_sem, 1)

            for i in range(4):
                job(4 * i, "T", hhi, hlo, ready=0 if i == 0 else None)
                if i:
                    turn_values(i - 1)
                job(4 * i + 1, "T", hhi, hlo)
                if i == 0:
                    pe.wait_ge(ab_in_sem, 16)
                    for k in range(KT):
                        m = mm(ps[3][0:16, 0:S], A(6144, 8, 16)[:, k, :], hf_a[:, k, :], k == 0, k == KT - 1)
                    m.then_inc(ab_ok_sem, 1)
                    pe.wait_ge(rel_in_sem, 16)
                    mm(ps[4][0:8, 0:S], A(8192, 8, parts=32), onehot, True, True).then_inc(bias_ps_sem, 1)
                for u in range(6 * i, 6 * i + 3):
                    ada(u)
                job(4 * i + 2, "T", hhi, hlo)
                sums(lambda t: sq_a[:, 0:2, :], 1, 512, qk_sq_sem, lambda t: 2 * i + 1)
                for u in range(6 * i + 3, 6 * i + 6):
                    ada(u)
                job(4 * i + 3, "T", hhi, hlo)
                if i == 0:
                    pe.wait_ge(scan_ok_sem, 1)
                    for c in range(2):
                        for r in range(2):
                            m = pe.transpose(ps[5][:, c * 32 + 16 * r:c * 32 + 16 * r + 16], r16[:, 3 + r, c * P:c * P + P], ident[0:16, 0:16])
                    m.then_inc(rowsT_ok_sem, 1)
                sums(lambda t: sq_a[:, 2:4, :], 1, 512, qk_sq_sem, lambda t: 2 * i + 2)
            turn_values(3)
            pe.wait_ge(qk_ok_sem, 8)
            pe.wait_ge(vb_ok_sem, 4)
            groups = [(0, 0), (0, 4), (1, 0), (1, 4)]
            for g, (c, h0) in enumerate(groups):
                pe.wait_ge(nt_ok_sem, g)
                sc = slice(c * P, c * P + P)
                for n in range(4):
                    h = h0 + n
                    o = slice(n * P, n * P + P)
                    mm(ps[3][:, o], ident[0:16, h:h + 1].to_broadcast([16, P]), r16[:, 3, sc], True, True)
                    mm(ps[4][:, o], ident[0:16, 8 + h:9 + h].to_broadcast([16, P]), r16[:, 4, sc], True, True)
                    mm(ps[5][:, o], kh[:, h, sc], kh[:, h, sc], True, True)
                    m = mm(ps[6][:, o], kh[:, h, sc], qh[:, h, sc], True, True)
                m.then_inc(delta_in_sem, 1)
            for c in range(2):
                for h0 in (0, 4):
                    b = ps[7 if h0 else 2]
                    pe.wait_ge(kcol_ok_sem, c)
                    if h0 == 0:
                        pe.wait_ge(ss_read_sem, own_ss[0])
                    else:
                        pe.wait_ge(mod_ok_sem, 4)
                    for n in range(4):
                        m = pe.transpose(b[:, n * P:n * P + P], kh[:, h0 + n, c * P:c * P + P], ident)
                m.then_inc(kT_ok_sem, 1)
            pe.wait_ge(kcol_ok_sem, 2)
            pe.wait_ge(nt_ok_sem, 4)
            for lv in range(LEVELS):
                n = 1 << lv
                for g in range(4):
                    b = ps[2 + g]
                    if lv:
                        pe.wait_ge(t_ok_sem, max(4 * (lv - 1) + g + 1, 0))
                    for m4 in range(4):
                        blk = 4 * g + m4
                        T = tt[:, blk, :].rearrange("p (a two b) -> p a two b", two=2, b=n)[:, :, 0, :]
                        m = mm(b[:, m4 * 64:m4 * 64 + 64], nt[:, blk, :], T if lv else ident.rearrange("p (a two) -> p a two", two=2)[:, :, 0], m4 == 0, True)
                    m.then_inc(p_ok_sem, 1)
                for g in range(4):
                    b = ps[2 + g]
                    if lv:
                        pe.wait_ge(u_ok_sem, max(4 * (lv - 1) + g + 1, 0))
                    pe.wait_ge(pe_v_sem, 4 * lv + g + 1)
                    for m4 in range(4):
                        m = mm(b[:, 256 + m4 * 64:256 + m4 * 64 + 64], uu[:, 4 * g + m4, :] if lv else ident, pp[:, g, m4 * 64:m4 * 64 + 64], m4 == 0, True)
                    m.then_inc(tp_ok_sem, 1)
                for g in range(4):
                    b = ps[6 + g % 2]
                    k = 4 * lv + g
                    pe.wait_ge(t_ok_sem, k + 1)
                    pe.wait_ge(u_ok_sem, max(k - 1, 0))
                    for m4 in range(4):
                        m = pe.transpose(b[:, m4 * P:m4 * P + P], tt[:, 4 * g + m4, :], ident)
                    m.then_inc(ut_ok_sem, 1)
            pe.wait_ge(u_ok_sem, 28)
            for g in range(2):
                for n in range(4):
                    h = 4 * g + n
                    m = mm(ps[2 + g][:, n * P:n * P + P], uu[:, h, :], vb[:, h, :], True, True)
                m.then_inc(un_ok_sem, 1)
            for g in range(2):
                for n in range(4):
                    h = 4 * g + n
                    m = mm(ps[4 + g][:, n * P:n * P + P], kbe[:, h, :], uu[:, 8 + h, :], True, True)
                m.then_inc(wt_ok_sem, 1)
            for g in range(2):
                pe.wait_ge(vn_ok_sem, g + 1)
                for n in range(4):
                    h = 4 * g + n
                    m = mm(ps[6 + g][:, n * P:n * P + P], kdec[:, h, :], vn0[:, h, :], True, True)
                m.then_inc(st_ok_sem, 1)
            for g in range(2):
                pe.wait_ge(stv_sem, g + 1)
                pe.wait_ge(wv_sem, g + 1)
                for n in range(4):
                    h = 4 * g + n
                    mm(ps[2 + g][:, n * P:n * P + P], uu[:, 8 + h, :], vb[:, 8 + h, :], n == 0, False)
                    m = mm(ps[2 + g][:, n * P:n * P + P], wt_[:, h, :], st1[:, h, :], False, n == 3)
                m.then_inc(vn1_ok_sem, 1)
            pe.wait_ge(egb_sem, 2)
            for i in range(4):
                b = ps[4 + i % 2]
                pe.wait_ge(vn1v_sem, i // 2 + 1)
                pe.wait_ge(o_split_sem, max(i - 1, 0))
                for n in range(2):
                    h = 2 * i + n
                    mm(b[:, n * S:n * S + P], vn0[:, h, :], qkd[:, h, :], n == 0, False)
                    mm(b[:, n * S + P:n * S + S], st1[:, h, :], qh[:, h, P:S], False, False)
                    m = mm(b[:, n * S + P:n * S + S], vn1[:, h, :], qkd[:, 8 + h, :], False, n == 1)
                m.then_inc(o_ok_sem, 1)
                sums(lambda t: osq[:, 2 * (i % 2):2 * (i % 2) + 2, :], 1, 512, o_sq_sem, lambda t: i + 1)
            pe.wait_ge(o_split_sem, 4)
            for J in range(JOB_OUT_A, JOB_B):
                job(J, "T", ohi, olo)

            def x_sums(n):
                sums(lambda t: xsq[:, t, :], 8, S, sq_ok_sem, lambda t: 4 * n + t // 2 + 1)

            def attend(J0, pairs, soft0, o0, h_q, h_kv, normed, ready, extra):
                def turn(i):
                    pe.wait_ge(p_soft_sem, soft0 + i + 1)
                    for hh in range(2):
                        pe.wait_ge(pT_v_sem, 2 * (soft0 + i) + hh)
                        for a, c0 in enumerate((256, 0, 128)):
                            m = pe.transpose(ps[5][:, a * P:a * P + P], ts[:, hh, c0:c0 + P], ident)
                        m.then_inc(pT_ok_sem, 1)

                def mix(i):
                    pe.wait_ge(pT_v_sem, 2 * (soft0 + i) + 2)
                    Jv = J0 + 4 * i + 3
                    pe.wait_ge(bank_free[Jv % 2], Jv // 2 + 1)
                    pe.wait_ge(o_split_sem, o0 + i)
                    for hh in range(2):
                        mm(ps[6][:, hh * S:hh * S + S], vs[:, 0, hh * P:hh * P + P], pt[:, hh, 0:256], hh == 0, False)
                        m = mm(ps[6][:, hh * S + P:hh * S + S], vs[:, 1, hh * P:hh * P + P], pt[:, hh, 256:384], False, hh == 1)
                    m.then_inc(o_ok_sem, 1)

                for i in range(pairs):
                    J = J0 + 4 * i
                    job(J, "T", *h_q, ready=ready[0] if i == 0 else None)
                    job(J + 1, "T", *h_kv, ready=ready[1] if i == 0 else None)
                    if i:
                        turn(i - 1)
                    extra(i, 0)
                    if normed:
                        sums(lambda t: sqb[:, 0:2, :], 1, 512, qk_sq_sem, lambda t: 8 + 2 * i + 1)
                    job(J + 2, "T", *h_q)
                    if i:
                        mix(i - 1)
                    extra(i, 1)
                    if normed:
                        sums(lambda t: sqb[:, 2:4, :], 1, 512, qk_sq_sem, lambda t: 8 + 2 * i + 2)
                    job(J + 3, "S", *h_kv)
                    if normed:
                        pe.wait_ge(qk_ok_sem, 8 + 2 * i + 2)
                    else:
                        for b in range(2):
                            pe.wait_ge(bank_free[b], J // 2 + 1)
                    pe.wait_ge(t_soft_sem, 2 * (soft0 + i))
                    for hh in range(2):
                        mm(ps[3 + hh][:, 0:256], qn[:, hh, P:S], kn[:, hh, :], True, False)
                        m = mm(ps[3 + hh][:, 256:384], qn[:, hh, 0:P], kn[:, hh, 0:P], False, True)
                        m.then_inc(s_ok_sem, 1)
                turn(pairs - 1)
                mix(pairs - 1)

            x_sums(1)

            def ada_b(i, part):
                for u in range(24 + 6 * i + 3 * part, 24 + 6 * i + 3 * part + 3):
                    ada(u)

            attend(JOB_B, 4, 0, 4, (ohi[:, 8:16, :], olo[:, 8:16, :]), (hhi, hlo), False, (4, 8), ada_b)
            pe.wait_ge(o_split_sem, 8)
            for J in range(JOB_OUT_B, JOB_C):
                job(J, "T", ohi, olo)
            x_sums(2)
            x_sums(3)

            def mix_c(h):
                for Jv in (JOB_C + 6 * h + 4, JOB_C + 6 * h + 5):
                    pe.wait_ge(bank_free[Jv % 2], Jv // 2 + 1)
                pe.wait_ge(sd_ok_sem, h + 1)
                pe.wait_ge(o_split_sem, 8 + h)
                for t in range(4):
                    b = ps[3 + t // 2]
                    c0 = (t % 2) * S
                    mm(b[:, c0:c0 + S], vs[:, 0, t * P:t * P + P], sd[:, 0:256], t % 2 == 0, False)
                    m = mm(b[:, c0 + P:c0 + S], vs[:, 1, t * P:t * P + P], sd[:, 256:384], False, t % 2 == 1)
                m.then_inc(o_ok_sem, 1)

            def sums_c(h):
                sums(lambda t: sq4[:, t, :], 4, S, o_sq_sem, lambda t: 4 + h + 1)

            for h in range(4):
                J = JOB_C + 6 * h
                job(J, "T", hhi, hlo, ready=12 if h == 0 else None)
                if h:
                    mix_c(h - 1)
                job(J + 1, "T", hhi, hlo)
                job(J + 2, "T", hhi, hlo)
                if h:
                    sums_c(h - 1)
                pe.wait_ge(rope_ok_sem, 2 * h + 2)
                pe.wait_ge(sd_ok_sem, h)
                for kt in range(2):
                    mm(ps[5][:, 0:256], kn[:, kt, 0:P], qn[:, kt, :], kt == 0, False)
                    m = mm(ps[5][:, 256:384], kn[:, kt, P:S], qn[:, kt, P:S], False, kt == 1)
                m.then_inc(sc_ok_sem, 1)
                job(J + 3, "T", hhi, hlo)
                job(J + 4, "S", hhi, hlo)
                job(J + 5, "S", hhi, hlo)
            mix_c(3)
            sums_c(3)
            pe.wait_ge(o_split_sem, 12)
            for J in range(JOB_OUT_C, JOB_D):
                job(J, "T", ohi, olo)
            x_sums(4)
            attend(JOB_D, 8, 4, 12, (hhi, hlo), (hhi, hlo), True, (16, 16), lambda i, p: None)
            pe.wait_ge(o_split_sem, 20)
            for J in range(JOB_OUT_D, N_JOBS):
                job(J, "T", ohi, olo)

        @block.scalar
        def _(act):
            ss_n = [0]

            def ln_exp_set():
                act.add_instruction(mybir.InstLoadActFuncSet(name=nc.get_next_instruction_name(), act_func_set_id=6, ins=[], outs=[]))

            def high(c):
                if c >= N_CHUNKS:
                    return
                for half in range(2):
                    unit = 2 * c + half
                    act.wait_ge(raw_in[c % RAW], 16 * (c // RAW + 1))
                    act.wait_ge(w_units_sem, max(unit + 1 - UNITS, 0))
                    act.wait_ge(lo_ok_sem, max(unit + 1 - UNITS, 0))
                    act.activation(whi[:, unit % UNITS, :, :], raw[:, c % RAW, 4 * half:4 * half + 4, :], ACT.Copy).then_inc(hi_ok_sem, 1)

            def at_job(J):
                for c in chunks_of(J):
                    high(c + 1)
                act.wait_ge(w_units_sem, 2 * chunks_of(J)[-1] + 2)

            def bank(J):
                return v2(pj[J % 2])

            def bank_taken(e, J):
                e.wait_ge(bank_free[J % 2], J // 2 + 1)

            def rsqrt(dst, width, scale):
                ss_n[0] += 1
                act.wait_ge(ss_ok_sem, ss_n[0])
                act.activation(dst, ssb[:, 0:width] if len(dst.shape) == 2 else v2(ssb), ACT.Ln, scale=scale, bias=epsc[:, 0:1]).then_inc(ss_read_sem, 1)
                act.wait_ge(ss_read_sem, ss_n[0])
                act.activation(dst, dst, ACT.Exp, scale=-0.5).then_inc(rs_ok_sem, 1)

            def split_h(prep, src, dst):
                for t in range(4):
                    act.wait_ge(hf_ok_sem, 8 * prep + 2 * t + 2)
                    act.activation(dst[:, 2 * t:2 * t + 2, :], src[:, 2 * t:2 * t + 2, :], ACT.Copy).then_inc(hh_ok_sem, 1)

            def square_x(J0):
                for n in range(4):
                    J = J0 + n
                    for c in chunks_of(J):
                        high(c + 1)
                    bank_taken(act, J)
                    act.activation(xsq[:, 2 * n:2 * n + 2, :], x[:, 2 * n:2 * n + 2, :], ACT.Square).then_inc(sq_ok_sem, 1)

            act.wait_ge(x_in_sem, 32)
            for t in range(4):
                act.activation(xsq_a[:, 2 * t:2 * t + 2, :], x[:, 2 * t:2 * t + 2, :], ACT.Square).then_inc(sq_ok_sem, 1)
            ln_exp_set()
            act.wait_ge(ones_ok_sem, 6)
            rsqrt(rs_a[:, 0, :], S, 1.0 / D)
            high(0)
            split_h(0, hf_a, hhi)
            act.wait_ge(cols_in_sem, 16)
            act.activation(sil[:, :], cols[:, COLS["cond"]:COLS["cond"] + KT], ACT.Silu).then_inc(sil_ok_sem, 1)

            for i in range(4):
                for k in range(4):
                    J = 4 * i + k
                    at_job(J)
                    if k < 3:
                        act.wait_ge(conv_ok_sem, max(6 * (i - 1) + 2 * k + 2, 0))
                        act.activation(pre[:, 2 * k:2 * k + 2, 3:259], bank(J), ACT.Copy).then_inc(bank_free[J % 2], 1)
                    else:
                        act.activation(zt[:, 2 * i:2 * i + 2, :], bank(J), ACT.Silu).then_inc(bank_free[J % 2], 1)
                    if k in (1, 2):
                        r = slice(2 * k - 2, 2 * k)
                        act.wait_ge(conv_ok_sem, 6 * i + 2 * k)
                        act.activation(raw_a[:, r, :], raw_a[:, r, :], ACT.Silu).then_inc(qk_raw_sem, 1)
                        act.wait_ge(qk_raw_sem, 2 * i + k)
                        act.activation(sq_a[:, r, :], raw_a[:, r, :], ACT.Square).then_inc(qk_sq_sem, 1)
                    if k == 2 and i == 0:
                        ln_exp_set()
                        act.wait_ge(rows_ok_sem, 1)
                        act.activation(r16[:, 1, :], r16[:, 1, :], ACT.Exp, scale=-1.0).then_inc(rowsv_sem, 1)
                        act.activation(rcol[:, :], cols[0:16, COLS["rows"] + 1:COLS["rows"] + 2], ACT.Exp)
                        act.wait_ge(rowsv_sem, 1)
                        act.activation(r16[:, 1, :], r16[:, 1, :], ACT.Ln, bias=epsc[0:16, 1:2]).then_inc(rowsv_sem, 1)
                        act.wait_ge(rows_ok_sem, 2)
                        act.activation(r16[:, 4, :], r16[:, 4, :], ACT.Exp).then_inc(scan_ok_sem, 1)
                    if k == 3:
                        act.wait_ge(conv_ok_sem, 6 * i + 6)
                        act.activation(vsil[:, :, :], vsil[:, :, :], ACT.Silu).then_inc(vsil_ok_sem, 1)
                        ln_exp_set()
                        rsqrt(rs_a[:, 0:2, :], 512, 1.0)
                        rsqrt(rs_a[:, 2:4, :], 512, 1.0)
            act.wait_ge(rowsT_ok_sem, 1)
            act.wait_ge(bcol_ok_sem, 1)
            act.activation(hc[:, 2, 8:16], hc[:, 0, 8:16], ACT.Exp).then_inc(ce_sem, 1)
            for g in range(4):
                act.wait_ge(e_pre_sem, g + 1)
                act.activation(ee[:, :, :], ee[:, :, :], ACT.Exp).then_inc(e_ok_sem, 1)
                if g >= 2:
                    act.wait_ge(nt_ok_sem, g)
                    act.activation(pp[:, 0:2, :], v2(ps[3]), ACT.Exp).then_inc(egb_sem, 1)
                if g == 1:
                    act.wait_ge(gl_ok_sem, 1)
                    act.activation(hc[:, 2, 0:8], hc[:, 3, 0:8], ACT.Exp).then_inc(ce_sem, 1)
            for lv in range(LEVELS):
                for g in range(4):
                    act.wait_ge(p_ok_sem, 4 * lv + g + 1)
                    act.activation(pp[:, g, :], ps[2 + g][:, 0:256], ACT.Copy).then_inc(pe_v_sem, 1)
                for g in range(4):
                    act.wait_ge(ut_ok_sem, 4 * lv + g + 1)
                    act.activation(uu[:, 4 * g:4 * g + 4, :], v2(ps[6 + g % 2], P), ACT.Copy).then_inc(u_ok_sem, 1)
            for g in range(2):
                act.wait_ge(un_ok_sem, g + 1)
                act.activation(vn0[:, 4 * g:4 * g + 4, :], v2(ps[2 + g], P), ACT.Copy).then_inc(vn_ok_sem, 1)
            for g in range(2):
                act.wait_ge(wt_ok_sem, g + 1)
                act.activation(wt_[:, 4 * g:4 * g + 4, :], v2(ps[4 + g], P), ACT.Copy).then_inc(wv_sem, 1)
            for g in range(2):
                act.wait_ge(vn1_ok_sem, g + 1)
                act.activation(vn1[:, 4 * g:4 * g + 4, :], v2(ps[2 + g], P), ACT.Copy).then_inc(vn1v_sem, 1)
            for i in range(4):
                p2 = slice(2 * (i % 2), 2 * (i % 2) + 2)
                act.wait_ge(o_ok_sem, i + 1)
                act.activation(osq[:, p2, :], v2(ps[4 + i % 2]), ACT.Square).then_inc(o_sq_sem, 1)
                act.wait_ge(o_split_sem, max(i - 1, 0))
                rsqrt(ors[:, p2, :], 512, 1.0 / DH)
            square_x(JOB_OUT_A)

            def attend(J0, pairs, soft0, v0, normed):
                def soft(i):
                    si = soft0 + i
                    for hh in range(2):
                        act.wait_ge(m_ok_sem, 2 * si + hh + 1)
                        for a, (c0, c1) in enumerate(((0, 256), (256, 384))):
                            k = 2 * hh + a
                            m = act.activation(ts[:, hh, c0:c1], ts[:, hh, c0:c1], ACT.Exp, bias=sm[:, 0, k:k + 1], accum_out=sm[:, 1, k:k + 1])
                        m.then_inc(e_soft_sem, 1)

                def turned(i):
                    for hh in range(2):
                        act.wait_ge(pT_ok_sem, 2 * (soft0 + i) + hh + 1)
                        act.activation(pt[:, hh, :], ps[5][:, 0:384], ACT.Copy).then_inc(pT_v_sem, 1)

                def split_c(J):
                    for c in chunks_of(J):
                        high(c + 1)

                for i in range(pairs):
                    J = J0 + 4 * i
                    split_c(J)
                    if i:
                        if normed:
                            ln_exp_set()
                        soft(i - 1)
                    for k, (raw_, to) in enumerate(((qraw, qn), (kraw, kn))):
                        if k:
                            split_c(J + 1)
                        act.wait_ge(w_units_sem, 2 * chunks_of(J + k)[-1] + 2)
                        if normed:
                            act.activation(sqb[:, 2 * k:2 * k + 2, :], bank(J + k), ACT.Square).then_inc(qk_sq_sem, 1)
                            act.wait_ge(qk_ok_sem, max(8 + 2 * (i - 1) + k + 1, 0))
                            act.activation(raw_[:, :, :], bank(J + k), ACT.Copy).then_inc(bank_free[(J + k) % 2], 1)
                        else:
                            act.wait_ge(s_ok_sem, 2 * (soft0 + i))
                            act.activation(to[:, :, :], bank(J + k), ACT.Copy).then_inc(bank_free[(J + k) % 2], 1)
                    if i:
                        turned(i - 1)
                    if normed:
                        if i == 0:
                            ln_exp_set()
                        rsqrt(rsb[:, 0:2, :], 512, 1.0 / DH)
                    split_c(J + 2)
                    split_c(J + 3)
                    if normed:
                        rsqrt(rsb[:, 2:4, :], 512, 1.0 / DH)
                    act.wait_ge(w_units_sem, 2 * chunks_of(J + 2)[-1] + 2)
                    act.activation(zs[:, 2 * (i % 2):2 * (i % 2) + 2, :], bank(J + 2), ACT.Silu).then_inc(bank_free[J % 2], 1)
                    act.wait_ge(w_units_sem, 2 * chunks_of(J + 3)[-1] + 2)
                    act.wait_ge(o_ok_sem, v0 + i)
                    act.activation(vs[:, :, 0:256], bank(J + 3), ACT.Copy).then_inc(bank_free[(J + 3) % 2], 1)
                ln_exp_set()
                soft(pairs - 1)
                turned(pairs - 1)

            ln_exp_set()
            rsqrt(rsb[:, 0, :], S, 1.0 / D)
            split_h(1, hf, ohi[:, 8:16, :])
            split_h(2, hf, hhi)
            attend(JOB_B, 4, 0, 4, False)
            square_x(JOB_OUT_B)
            ln_exp_set()
            rsqrt(rsb[:, 0, :], S, 1.0 / D)
            for t in range(4):
                act.wait_ge(xn_ok_sem, t + 1)
                act.activation(xsq[:, 2 * t:2 * t + 2, :], x[:, 2 * t:2 * t + 2, :], ACT.Square).then_inc(sq_ok_sem, 1)
            rsqrt(rsb[:, 0, :], S, 1.0 / D)
            split_h(3, hf, hhi)
            act.wait_ge(fin_rope_sem, 1)
            act.activation(sint, tr1, ACT.Sin)
            act.activation(cost, tr2, ACT.Sin).then_inc(fin_rope_sem, 1)
            for h in range(5):
                J = JOB_C + 6 * h
                if h < 4:
                    high(J + 1)
                    high(J + 2)
                if h < 4:
                    high(J + 3)
                if h:
                    act.wait_ge(o_ok_sem, 8 + h)
                    act.activation(sq4[:, 0:2, :], v2(ps[3]), ACT.Square)
                    act.activation(sq4[:, 2:4, :], v2(ps[4]), ACT.Square).then_inc(o_sq_sem, 1)
                if h < 4:
                    act.wait_ge(w_units_sem, 2 * (J + 2) + 2)
                    act.activation(zs_c[:, 4 * (h % 2):4 * (h % 2) + 2, :], bank(J + 2), ACT.Silu).then_inc(bank_free[J % 2], 1)
                    high(J + 4)
                    act.wait_ge(w_units_sem, 2 * (J + 3) + 2)
                    act.activation(zs_c[:, 4 * (h % 2) + 2:4 * (h % 2) + 4, :], bank(J + 3), ACT.Silu).then_inc(bank_free[(J + 1) % 2], 1)
                if h:
                    ln_exp_set()
                    rsqrt(rsb[:, 0, :], S, 1.0 / 512)
                if h < 4:
                    for k in range(2):
                        high(J + 5 + k)
                        act.wait_ge(w_units_sem, 2 * (J + 4 + k) + 2)
                        act.wait_ge(o_ok_sem, 8 + h)
                        act.activation(vs[:, :, 256 * k:256 * k + 256], bank(J + 4 + k), ACT.Copy).then_inc(bank_free[(J + k) % 2], 1)
            square_x(JOB_OUT_C)
            rsqrt(rsb[:, 0, :], S, 1.0 / D)
            split_h(4, hf, hhi)
            attend(JOB_D, 8, 4, 12, True)
            for J in range(JOB_OUT_D, N_JOBS):
                for c in chunks_of(J):
                    high(c + 1)

        @block.vector
        def _(dve):
            steps = [0]

            def own(ins):
                steps[0] += 1
                ins.then_inc(dve_own_sem, 1)

            rs_n = [0]

            def low(c):
                if c >= N_CHUNKS:
                    return
                for half in range(2):
                    unit = 2 * c + half
                    dve.wait_ge(hi_ok_sem, unit + 1)
                    dve.tensor_tensor(wlo[:, unit % UNITS, :, :], raw[:, c % RAW, 4 * half:4 * half + 4, :],
                                      whi[:, unit % UNITS, :, :].bitcast(F32), ALU.subtract).then_inc(lo_ok_sem, 1)

            def lows(J):
                for c in chunks_of(J):
                    low(c + 1)

            def sums_done(J):
                dve.wait_ge(w_units_sem, 2 * chunks_of(J)[-1] + 2)

            def bank(J):
                return v2(pj[J % 2])

            def next_rs():
                rs_n[0] += 1
                dve.wait_ge(rs_ok_sem, rs_n[0])

            def wide(v, n):
                return v.unsqueeze(1).to_broadcast([P, n, v.shape[-1]])

            def prepare(prep, gain, shift, f, rs, hi, lo):
                def lo_part(p):
                    dve.wait_ge(hh_ok_sem, 4 * prep + p + 1)
                    r = slice(2 * p, 2 * p + 2)
                    dve.tensor_tensor(lo[:, r, :], f[:, r, :], hi[:, r, :].bitcast(F32), ALU.subtract).then_inc(h_ok_sem, 1)

                dve.wait_ge(h_ok_sem, 4 * prep)
                for t in range(KT):
                    m = dve.scalar_tensor_tensor(out=f[:, t, :], in0=x[:, t, :], scalar=gain(t), in1=rs, op0=ALU.mult, op1=ALU.mult)
                    if shift is not None:
                        own(m)
                        dve.wait_ge(dve_own_sem, steps[0])
                        m = dve.tensor_scalar(f[:, t, :], f[:, t, :], shift(t), None, ALU.add)
                    m.then_inc(hf_ok_sem, 1)
                    if t >= 3 and t % 2:
                        lo_part(t // 2 - 1)
                lo_part(3)

            def split_o(src, tile, n):
                dve.wait_ge(dve_own_sem, steps[0])
                r = slice(tile, tile + n)
                own(dve.tensor_copy(ohi[:, r, :], src))
                dve.wait_ge(dve_own_sem, steps[0])
                return dve.tensor_tensor(olo[:, r, :], src, ohi[:, r, :].bitcast(F32), ALU.subtract)

            dve.wait_ge(cols_in_sem, 16)
            next_rs()
            low(0)
            prepare(0, lambda t: col("a_norm", t), None, hf_a, rs_a[:, 0, :], hhi, hlo)

            def conv(i, k, dst):
                dve.wait_ge(qk_ok_sem, 2 * i)
                for t in range(2):
                    tile = 8 * k + 2 * i + t
                    u = pre[:, 2 * k + t, :]
                    own(dve.tensor_scalar(dst[:, t, :], u[:, 3:259], col("conv", 4 * tile + 3), None, ALU.mult))
                    for j in (2, 1, 0):
                        dve.wait_ge(dve_own_sem, steps[0])
                        m = dve.scalar_tensor_tensor(out=dst[:, t, :], in0=u[:, j:j + S], scalar=col("conv", 4 * tile + j), in1=dst[:, t, :], op0=ALU.mult, op1=ALU.add)
                        if j:
                            own(m)
                    m.then_inc(conv_ok_sem, 1)

            def take_mod(i):
                dve.wait_ge(ada_used_sem, 6 * i + 6)
                a0 = COLS["ada_b"] + 6 * i
                dve.tensor_tensor(mod[:, 6 * i:6 * i + 6], ps[7][:, 0:6], cols[:, a0:a0 + 6], ALU.add).then_inc(mod_ok_sem, 1)

            def take_values(i):
                dve.wait_ge(vT_ok_sem, i + 1)
                for n in range(4):
                    h, c = 2 * i + n // 2, n % 2
                    m = dve.tensor_scalar(vb[:, 8 * c + h, :], ps[3][:, n * P:n * P + P], hc[:, 1, 8 * c + h:8 * c + h + 1], None, ALU.mult)
                m.then_inc(vb_ok_sem, 1)

            dve.wait_ge(ones_ok_sem, 6)
            for i in range(4):
                for k in range(4):
                    J = 4 * i + k
                    lows(J)
                    if k < 3:
                        dve.wait_ge(bank_free[J % 2], J // 2 + 1)
                        if k == 2:
                            dve.wait_ge(vT_ok_sem, i)
                        conv(i, k, raw_a[:, 2 * k:2 * k + 2, :] if k < 2 else vsil)
                    if k == 1 and i:
                        take_values(i - 1)
                    if k == 1 and i == 0:
                        dve.wait_ge(ab_ok_sem, 1)
                        own(dve.tensor_scalar(r16[:, 0, :], ps[3][0:16, 0:S], cols[0:16, COLS["rows"]:COLS["rows"] + 1], None, ALU.add))
                        dve.wait_ge(dve_own_sem, steps[0])
                        dve.scalar_tensor_tensor(out=r16[:, 1, :], in0=r16[:, 0, :], scalar=-1.0, in1=r16[:, 0, :], op0=ALU.mult, op1=ALU.max).then_inc(rows_ok_sem, 1)
                        dve.wait_ge(bias_ps_sem, 1)
                        dve.tensor_copy(fb[0:8, 0:S], ps[4][0:8, 0:S]).then_inc(bias_sb_sem, 1)
                    if k == 2 and i == 0:
                        dve.wait_ge(rowsv_sem, 2)
                        own(dve.scalar_tensor_tensor(out=r16[:, 2, :], in0=r16[:, 0, :], scalar=0.0, in1=r16[:, 1, :], op0=ALU.max, op1=ALU.add))
                        dve.wait_ge(dve_own_sem, steps[0])
                        dve.tensor_tensor(r16[:, 4, :], r16[:, 0, :], r16[:, 2, :], ALU.subtract)
                        own(dve.tensor_scalar(r16[:, 1, :], r16[:, 2, :], rcol[:, 0:1], -1.0, ALU.mult, ALU.mult))
                        dve.wait_ge(dve_own_sem, steps[0])
                        for c in range(2):
                            cs = slice(c * P, c * P + P)
                            m = dve.tensor_tensor_scan(r16[:, 3, cs], r16[:, 5, cs], r16[:, 1, cs], 0.0, ALU.mult, ALU.add)
                        m.then_inc(rows_ok_sem, 1)
                    if k == 3:
                        if i == 0:
                            dve.wait_ge(rowsT_ok_sem, 1)
                            for c in range(2):
                                dve.tensor_copy(hc[:, 0, 8 * c:8 * c + 8], ps[5][:, 32 * c:32 * c + 8])
                                m = dve.tensor_copy(hc[:, 1, 8 * c:8 * c + 8], ps[5][:, 32 * c + 24:32 * c + 32])
                            m.then_inc(bcol_ok_sem, 1)
                            dve.wait_ge(bcol_ok_sem, 1)
                        take_mod(i)
                        for n, (to, sc) in enumerate(((qh, DH ** -0.5), (kh, 1.0))):
                            next_rs()
                            dve.scalar_tensor_tensor(out=to[:, 2 * i:2 * i + 2, :], in0=raw_a[:, 2 * n:2 * n + 2, :], scalar=sc, in1=rs_a[:, 2 * n:2 * n + 2, :], op0=ALU.mult, op1=ALU.mult).then_inc(qk_ok_sem, 1)
            take_values(3)
            groups = [(0, 0), (0, 4), (1, 0), (1, 4)]
            for g, (c, h0) in enumerate(groups):
                dve.wait_ge(delta_in_sem, g + 1)
                dve.wait_ge(nt_ok_sem, g)
                for n in range(4):
                    h = h0 + n
                    m = dve.scalar_tensor_tensor(out=ee[:, n, :], in0=ps[3][:, n * P:n * P + P], scalar=hc[:, 0, 8 * c + h:8 * c + h + 1], in1=causal, op0=ALU.subtract, op1=ALU.add)
                m.then_inc(e_pre_sem, 1)
                b4 = slice(4 * g, 4 * g + 4)
                if c == 0:
                    own(dve.tensor_copy(hc[:, 3, h0:h0 + 4], v2(ps[3], P)[:, :, P - 1]))
                    if g == 1:
                        dve.wait_ge(dve_own_sem, steps[0])
                        dve.tensor_tensor(hc[:, 3, 0:8], hc[:, 3, 0:8], hc[:, 0, 0:8], ALU.subtract).then_inc(gl_ok_sem, 1)
                own(dve.tensor_tensor(nt[:, b4, :], v2(ps[4], P), wide(strict, 4), ALU.mult))
                dve.wait_ge(e_ok_sem, g + 1)
                own(dve.tensor_tensor(ke[:, :, :], v2(ps[5], P), ee[:, :, :], ALU.mult))
                own(dve.tensor_tensor(qkd[:, b4, :], v2(ps[6], P), ee[:, :, :], ALU.mult))
                dve.wait_ge(dve_own_sem, steps[0])
                if c == 1:
                    dve.wait_ge(egb_sem, max(g - 1, 0))
                    dve.tensor_tensor(qh[:, h0:h0 + 4, P:S], qh[:, h0:h0 + 4, P:S], pp[:, 0:2, :].rearrange("p a (b c) -> p (a b) c", b=2), ALU.mult)
                dve.tensor_tensor(nt[:, b4, :], nt[:, b4, :], ke[:, :, :], ALU.mult).then_inc(nt_ok_sem, 1)
            dve.wait_ge(mask_ok_sem, LEVELS)
            dve.wait_ge(ce_sem, 2)
            own(dve.scalar_tensor_tensor(out=hc[:, 4, 8:16], in0=hc[:, 1, 8:16], scalar=-1.0, in1=hc[:, 2, 8:16], op0=ALU.mult, op1=ALU.mult))
            dve.wait_ge(dve_own_sem, steps[0])
            for c, (to, w) in enumerate(((kdec, hc[:, 2, 0:8]), (kbe, hc[:, 4, 8:16]))):
                dve.wait_ge(kT_ok_sem, c + 1)
                for h in range(8):
                    m = dve.tensor_scalar(to[:, h, :], ps[2 if h < 4 else 7][:, (h % 4) * P:(h % 4) * P + P], w[:, h:h + 1], None, ALU.mult)
                m.then_inc(kcol_ok_sem, 1)
            own(dve.tensor_copy(tt[:, :, :], wide(ident, 16)))
            dve.wait_ge(dve_own_sem, steps[0])
            for lv in range(LEVELS):
                n = 1 << lv
                for g in range(4):
                    dve.wait_ge(tp_ok_sem, 4 * lv + g + 1)
                    T = tt[:, 4 * g:4 * g + 4, :].rearrange("p g c -> p (g c)").rearrange("p (a two b) -> p a two b", two=2, b=n)[:, :, 0, :]
                    dve.copy_predicated(T, lmask[:, lv, :].rearrange("p (a b) -> p a b", b=n), ps[2 + g][:, 256:512].rearrange("p (a b) -> p a b", b=n)).then_inc(t_ok_sem, 1)
            for g in range(2):
                dve.wait_ge(st_ok_sem, g + 1)
                dve.tensor_copy(st1[:, 4 * g:4 * g + 4, :], v2(ps[6 + g], P)).then_inc(stv_sem, 1)
            for i in range(4):
                p2 = slice(2 * (i % 2), 2 * (i % 2) + 2)
                next_rs()
                dve.wait_ge(o_split_sem, i)
                own(dve.scalar_tensor_tensor(out=oof[:, :, :], in0=v2(ps[4 + i % 2]), scalar=col("a_out"), in1=ors[:, p2, :], op0=ALU.mult, op1=ALU.mult))
                dve.wait_ge(dve_own_sem, steps[0])
                own(dve.tensor_tensor(oof[:, :, :], oof[:, :, :], zt[:, 2 * i:2 * i + 2, :], ALU.mult))
                split_o(oof[:, :, :], 2 * i, 2).then_inc(o_split_sem, 1)

            def add_x(J0, gate=None):
                for n in range(4):
                    J = J0 + n
                    lows(J)
                    sums_done(J)
                    if gate is None:
                        dve.tensor_tensor(x[:, 2 * n:2 * n + 2, :], bank(J), x[:, 2 * n:2 * n + 2, :], ALU.add).then_inc(bank_free[J % 2], 1)
                    else:
                        for t in range(2):
                            k = 2 * n + t
                            m = dve.scalar_tensor_tensor(out=x[:, k, :], in0=bank(J)[:, t, :], scalar=mod[:, gate + k:gate + k + 1], in1=x[:, k, :], op0=ALU.mult, op1=ALU.add)
                        m.then_inc(bank_free[J % 2], 1)

            def attend(J0, pairs, soft0, bias, normed, modded):
                def scores_in(i):
                    si = soft0 + i
                    for hh in range(2):
                        dve.wait_ge(s_ok_sem, 2 * si + hh + 1)
                        dve.wait_ge(pT_ok_sem, max(2 * si + hh - 1, 0))
                        own_ts = dve.scalar_tensor_tensor(out=ts[:, hh, :], in0=ps[3 + hh][:, 0:384], scalar=DH ** -0.5, in1=bias[:, 2 * i + hh, :], op0=ALU.mult, op1=ALU.add)
                        own_ts.then_inc(t_soft_sem, 1)
                        dve.wait_ge(t_soft_sem, 2 * si + hh + 1)
                        for a, (c0, c1) in enumerate(((0, 256), (256, 384))):
                            m = dve.tensor_reduce(sm[:, 0, 2 * hh + a:2 * hh + a + 1], ts[:, hh, c0:c1], AX.X, ALU.max, negate=True)
                        m.then_inc(m_ok_sem, 1)

                def scale_p(i):
                    for hh in range(2):
                        dve.wait_ge(e_soft_sem, 2 * (soft0 + i) + hh + 1)
                        dve.wait_ge(p_soft_sem, soft0 + i)
                        own(dve.reciprocal(sm[:, 2, 2 * hh:2 * hh + 2], sm[:, 1, 2 * hh:2 * hh + 2]))
                        dve.wait_ge(dve_own_sem, steps[0])
                        for a, (c0, c1) in enumerate(((0, 256), (256, 384))):
                            m = dve.tensor_scalar(ts[:, hh, c0:c1], ts[:, hh, c0:c1], sm[:, 2, 2 * hh + a:2 * hh + a + 1], None, ALU.mult)
                    m.then_inc(p_soft_sem, 1)

                def finish(i):
                    dve.wait_ge(o_ok_sem, soft_o + i + 1)
                    dve.wait_ge(o_split_sem, soft_o + i)
                    dve.wait_ge(bank_free[J0 % 2], (J0 + 4 * i + 2) // 2 + 1)
                    own(dve.tensor_tensor(of[:, :, :], v2(ps[6]), zs[:, 2 * (i % 2):2 * (i % 2) + 2, :], ALU.mult))
                    split_o(of[:, :, :], 2 * i, 2).then_inc(o_split_sem, 1)

                soft_o = 4 if not normed else 12
                for i in range(pairs):
                    J = J0 + 4 * i
                    lows(J)
                    if i:
                        scores_in(i - 1)
                        scale_p(i - 1)
                    lows(J + 1)
                    lows(J + 2)
                    if normed:
                        next_rs()
                        dve.wait_ge(s_ok_sem, 2 * (soft0 + i))
                        dve.scalar_tensor_tensor(out=qn[:, :, :], in0=qraw[:, :, :], scalar=col("att_q"), in1=rsb[:, 0:2, :], op0=ALU.mult, op1=ALU.mult).then_inc(qk_ok_sem, 1)
                    lows(J + 3)
                    if normed:
                        next_rs()
                        dve.scalar_tensor_tensor(out=kn[:, :, :], in0=kraw[:, :, :], scalar=col("att_k"), in1=rsb[:, 2:4, :], op0=ALU.mult, op1=ALU.mult).then_inc(qk_ok_sem, 1)
                    if i:
                        finish(i - 1)
                    if modded:
                        take_mod(4 + i)
                scores_in(pairs - 1)
                scale_p(pairs - 1)
                finish(pairs - 1)

            add_x(JOB_OUT_A)
            next_rs()
            prepare(1, lambda t: col("b_norm", t), None, hf, rsb[:, 0, :], ohi[:, 8:16, :], olo[:, 8:16, :])
            prepare(2, lambda t: col("kv_norm", t), None, hf, rsb[:, 0, :], hhi, hlo)
            dve.wait_ge(bias_ok_sem, 32)
            attend(JOB_B, 4, 0, A(bias_at, 8, 384), False, True)
            add_x(JOB_OUT_B)
            next_rs()
            for t in range(KT):
                m = dve.scalar_tensor_tensor(out=x[:, t, :], in0=x[:, t, :], scalar=col("final_norm", t), in1=rsb[:, 0, :], op0=ALU.mult, op1=ALU.mult)
                if t % 2:
                    m.then_inc(xn_ok_sem, 1)
            for l in range(2):
                own(dve.scalar_tensor_tensor(out=gsc[:, 8 * l:8 * l + 8], in0=mod[:, 24 * l + 8:24 * l + 16], scalar=1.0, in1=cols[:, COLS["norm2"] + 8 * l:COLS["norm2"] + 8 * l + 8], op0=ALU.add, op1=ALU.mult))
            dve.wait_ge(pos_in_sem, 16)
            own(dve.tensor_copy(ang, posi))
            dve.wait_ge(dve_own_sem, steps[0])
            own(dve.tensor_scalar(ang, ang, col("inv_freq"), None, ALU.mult))
            dve.wait_ge(dve_own_sem, steps[0])
            own(dve.tensor_scalar(tr1, ang, float(1.0 / (2 * np.pi)), 12582912.0, ALU.mult, ALU.add))
            dve.wait_ge(dve_own_sem, steps[0])
            own(dve.tensor_scalar(tr1, tr1, 12582912.0, None, ALU.subtract))
            two_pi = 2 * np.pi
            c1 = 6.28125
            c2 = float(np.float32(np.round((two_pi - c1) * 2 ** 21) / 2 ** 21))
            c3 = float(two_pi - c1 - c2)
            for cc in (c1, c2, c3):
                dve.wait_ge(dve_own_sem, steps[0])
                own(dve.scalar_tensor_tensor(out=ang, in0=tr1, scalar=-cc, in1=ang, op0=ALU.mult, op1=ALU.add))
            dve.wait_ge(dve_own_sem, steps[0])
            lim = 3.1415925
            own(dve.tensor_scalar(tr1, ang, lim, -lim, ALU.min, ALU.max))
            own(dve.tensor_scalar(ang, ang, float(np.pi / 2), None, ALU.add))
            dve.wait_ge(dve_own_sem, steps[0])
            own(dve.tensor_scalar(tr2, ang, float(np.pi), -two_pi, ALU.is_gt, ALU.mult))
            dve.wait_ge(dve_own_sem, steps[0])
            own(dve.tensor_tensor(tr2, tr2, ang, ALU.add))
            dve.wait_ge(dve_own_sem, steps[0])
            dve.tensor_scalar(tr2, tr2, lim, -lim, ALU.min, ALU.max).then_inc(fin_rope_sem, 1)
            next_rs()
            prepare(3, lambda t: gsc[:, t:t + 1], lambda t: mod[:, t:t + 1], hf, rsb[:, 0, :], hhi, hlo)
            dve.wait_ge(fin_rope_sem, 2)
            dve.wait_ge(dtab_in_sem, 16)

            def finish_c(h):
                next_rs()
                dve.wait_ge(o_split_sem, 8 + h)
                for b in range(2):
                    if b:
                        dve.wait_ge(dve_own_sem, steps[0])
                    own(dve.tensor_tensor(of[:, :, :], v2(ps[3 + b]), wide(rsb[:, 0, :], 2), ALU.mult))
                    dve.wait_ge(dve_own_sem, steps[0])
                    for t in range(2):
                        k = 2 * b + t
                        own(dve.scalar_tensor_tensor(out=of[:, t, :], in0=of[:, t, :], scalar=col("ret_gn", 4 * h + k), in1=zs_c[:, 4 * (h % 2) + k, :], op0=ALU.mult, op1=ALU.mult))
                    m = split_o(of[:, :, :], 4 * h + 2 * b, 2)
                    if b == 0:
                        own(m)
                m.then_inc(o_split_sem, 1)

            for h in range(4):
                J = JOB_C + 6 * h
                for k, to in enumerate((qn, kn)):
                    lows(J + k)
                    sums_done(J + k)
                    dve.wait_ge(sc_ok_sem, h)
                    dve.wait_ge(rope_ok_sem, 2 * h + k)
                    own(dve.tensor_tensor(rt1[:, :, :], bank(J + k), wide(cost, 2), ALU.mult))
                    dve.tensor_tensor(rt2[:, :, :], bank(J + k), wide(sint, 2), ALU.mult).then_inc(bank_free[(J + k) % 2], 1)
                    dve.wait_ge(dve_own_sem, steps[0])
                    dve.wait_ge(bank_free[(J + k) % 2], (J + k) // 2 + 1)
                    dve.tensor_tensor(to[:, 0, :], rt1[:, 0, :], rt2[:, 1, :], ALU.subtract)
                    dve.tensor_tensor(to[:, 1, :], rt2[:, 0, :], rt1[:, 1, :], ALU.add).then_inc(rope_ok_sem, 1)
                lows(J + 2)
                lows(J + 3)
                dve.wait_ge(sc_ok_sem, h + 1)
                dve.wait_ge(o_ok_sem, 8 + h)
                dve.tensor_tensor(sd, ps[5][:, 0:384], dmat[:, h, :], ALU.mult).then_inc(sd_ok_sem, 1)
                lows(J + 4)
                if h:
                    finish_c(h - 1)
                lows(J + 5)
            finish_c(3)
            add_x(JOB_OUT_C, gate=16)
            next_rs()
            prepare(4, lambda t: gsc[:, 8 + t:9 + t], lambda t: mod[:, 24 + t:25 + t], hf, rsb[:, 0, :], hhi, hlo)
            dve.wait_ge(bias_ok_sem, 96)
            dve.wait_ge(boot_sem, 4)
            attend(JOB_D, 8, 4, A(bias_at, 16, 384), True, False)
            add_x(JOB_OUT_D, gate=40)


def shape_tables():
    import math
    cst = np.zeros((P, N_CONST), np.float32)
    cst[:, C_IDENT:C_IDENT + P] = np.eye(P)
    j, i = np.arange(P)[:, None], np.arange(P)[None, :]
    cst[:, C_CAUSAL:C_CAUSAL + P] = np.where(i >= j, 0, NEG)
    cst[:, C_STRICT:C_STRICT + P] = np.where(i > j, -1, 0)
    n = np.arange(S)
    nf = np.maximum(n, 1).astype(np.float32)
    large = 16 + (np.log(nf / np.float32(16)) / np.float32(math.log(2048 / 16)) * np.float32(16)).astype(np.int32)
    bucket = np.where(n < 16, n, np.minimum(large, 31))
    for t in range(S):
        cst[bucket[S - 1 - t], C_ONEHOT + t] = 1
    lmask = np.zeros((P, LEVELS, 64), np.int32)
    for lv in range(LEVELS):
        w = 1 << lv
        left = [c for c in range(P) if (c // w) % 2 == 0]
        for k, c in enumerate(left):
            lmask[c // (2 * w) * 2 * w + w:c // (2 * w) * 2 * w + 2 * w, lv, k] = 1
    dtab = np.zeros((P, 4, 384), np.float32)
    lg = np.log(1.0 - 2.0 ** (-5.0 - np.arange(4, dtype=np.float64)))
    jj, ii = np.arange(S)[:, None], np.arange(S)[None, :]
    for h in range(4):
        full = np.where(jj // 64 <= ii // 64, np.exp(lg[h] * np.abs(ii - jj)), 0) / 16
        dtab[:, h, 0:256] = full[0:P]
        dtab[:, h, 256:384] = full[P:, P:]
    inv = (1.0 / (np.float32(10000.0) ** (np.arange(0, 256, 2, dtype=np.float32) / np.float32(256)))).astype(np.float32)
    return cst, lmask.reshape(P, LEVELS * 64), dtab, inv


def laid_out(z):
    def split(w, rows0, cols0):
        return w[rows0:rows0 + D, cols0:cols0 + 256].reshape(KT, P, 256).transpose(1, 0, 2).reshape(P, KT * 256)

    chunks = []
    w = z["a_w_in"][0]
    for i in range(4):
        for k in range(4):
            chunks.append(split(w, 0, 1024 * k + 256 * i))
    for n in range(4):
        chunks.append(split(z["a_w_out"][0], 0, 256 * n))
    for i in range(4):
        chunks.append(split(z["b_w_in"][0], 0, 256 * i))
        chunks.append(split(z["w_kv"], 0, 256 * i))
        chunks.append(split(z["b_w_in"][0], 0, 1024 + 256 * i))
        chunks.append(split(z["w_kv"], 0, 1024 + 256 * i))
    for n in range(4):
        chunks.append(split(z["b_w_out"][0], 0, 256 * n))
    w = z["ret_w_in_2"][0]
    for h in range(4):
        for c0 in (256 * h, 1024 + 256 * h, 4096 + 512 * h, 4096 + 512 * h + 256, 2048 + 512 * h, 2048 + 512 * h + 256):
            chunks.append(split(w, 0, c0))
    for n in range(4):
        for hf in range(2):
            chunks.append(split(z["ret_w_out_2"][0], D * hf, 256 * n))
    w = z["att_w_in_2"][0]
    for i in range(8):
        for c0 in (0, 2048, 6144, 4096):
            chunks.append(split(w, 0, c0 + 256 * i))
    for n in range(4):
        for hf in range(2):
            chunks.append(split(z["att_w_out_2"][0], D * hf, 256 * n))
    ada = []
    for l in range(2):
        for u in range(24):
            ada.append(z["ada_w_2"][l][:, 128 * u:128 * u + 128].reshape(KT, P, 128).transpose(1, 0, 2).reshape(P, KT * 128))

    def down(v):
        return v.reshape(-1, P).T

    cst, lmask, dtab, inv = shape_tables()
    rows = np.zeros((P, 2), np.float32)
    rows[0:8, 0] = z["a_dt_bias"][0]
    rows[0:8, 1] = z["a_log"][0]
    conv = z["a_conv_w"][0].reshape(4, 24, P).transpose(2, 1, 0).reshape(P, 96)
    cols = np.concatenate([down(z["a_norm_g"][0]), down(z["kv_norm_g"]), down(z["b_norm_g"][0]), down(z["final_norm_g"]),
                           down(z["norm_g_2"].reshape(-1)), down(z["ret_gn_g_2"][0]), down(z["att_q_g_2"][0]),
                           down(z["att_k_g_2"][0]), down(z["a_out_norm_g"][0]), conv, down(z["c_2"][0]),
                           down(z["ada_b_2"].reshape(-1)), rows, inv[:, None]], axis=1)
    return {
        "x_t": z["x"][0].T.reshape(KT, P, S).transpose(1, 0, 2),
        "weights": np.stack(chunks),
        "ada": np.stack(ada),
        "cols": cols,
        "consts": cst,
        "join_masks": lmask,
        "w_ab": z["a_w_in"][0][:, 4096:4112].reshape(KT, P, 16).transpose(1, 0, 2),
        "rel_b": z["rel_bias"],
        "rel_d": z["att_rel_bias_2"][0][:, ::-1],
        "decay": dtab,
        "positions": z["positions_2"],
    }


def kernel(**inputs):
    import concourse.bacc as _bacc
    from concourse.bass_utils import run_bass_kernel_spmd as _run

    z = {k: np.asarray(v) for k, v in inputs.items()}
    arrays = {k: np.ascontiguousarray(v) for k, v in laid_out(z).items()}
    nc = _bacc.Bacc("TRN2", target_bir_lowering=False, num_devices=1)
    aps = [nc.dram_tensor(k, v.shape, mybir.dt.from_np(v.dtype), kind="ExternalInput").ap() for k, v in arrays.items()]
    out = nc.dram_tensor("out_t", (P, KT, S), F32, kind="ExternalOutput").ap()
    scr_b = nc.dram_tensor("bias_rows_b", (P, 8, 512), F32, kind="Internal").ap()
    scr_d = nc.dram_tensor("bias_rows_d", (P, 16, 512), F32, kind="Internal").ap()
    x_in, wts, ada_w, cols_in, const_in, lmask_in, w_ab, rel_b, rel_d, dtab, pos = aps
    two_blocks(nc, x_in, wts, ada_w, cols_in, const_in, lmask_in, w_ab, rel_b, rel_d, dtab, pos, out, scr_b, scr_d)
    r = _run(nc, [arrays], core_ids=[0])
    got = r.results[0]["out_t"]
    return np.ascontiguousarray(got.transpose(2, 1, 0).reshape(1, S, D))
```

```python
import numpy as np
import concourse.bass as bass
from concourse import mybir
from contextlib import ExitStack

P = 128
S = 256
D = 1024
KT = D // P
HEADS = 8
DH = 128
EPS = 1e-6
F32 = mybir.dt.float32
F32R = mybir.dt.float32r
I32 = mybir.dt.int32
U8 = mybir.dt.uint8
ALU = mybir.AluOpType
ACT = mybir.ActivationFunctionType
AX = mybir.AxisListType
NEG = -1e30

COLS = {}
_at = 0
for _name, _n in (("a_norm", 8), ("kv_norm", 8), ("b_norm", 8), ("final_norm", 8), ("norm2", 16), ("ret_gn", 16),
                  ("att_q", 1), ("att_k", 1), ("a_out", 1), ("conv", 96), ("cond", 8), ("ada_b", 48), ("rows", 2),
                  ("inv_freq", 1)):
    COLS[_name] = _at
    _at += _n
N_COLS = _at
C_IDENT, C_CAUSAL, C_STRICT, C_ONEHOT, N_CONST = 0, 128, 256, 384, 640
LEVELS = 7
N_CHUNKS = 112
RAW = 3
UNITS = 4
ADA_UNITS = 48

JOB_OUT_A, JOB_B, JOB_OUT_B, JOB_C, JOB_OUT_C, JOB_D, JOB_OUT_D, N_JOBS = 16, 20, 36, 40, 64, 68, 100, 104


def chunks_of(job):
    if job < JOB_OUT_C:
        return [job]
    if job < JOB_D:
        return [JOB_OUT_C + 2 * (job - JOB_OUT_C) + h for h in range(2)]
    if job < JOB_OUT_D:
        return [job + 4]
    return [JOB_OUT_D + 4 + 2 * (job - JOB_OUT_D) + h for h in range(2)]


def two_blocks(nc, x_in, wts, ada_w, cols_in, const_in, lmask_in, w_ab, rel_b, rel_d, dtab, pos, out,
               scr_b, scr_d):
    ctx = ExitStack()
    with ctx:
        def sb(name, shape, dt=F32):
            return ctx.enter_context(nc.sbuf_tensor(name, shape, dt))

        def sem(name):
            return ctx.enter_context(nc.semaphore(name))

        raw = sb("raw", [P, RAW, KT, 256])
        whi = sb("whi", [P, UNITS, 4, 256], F32R)
        wlo = sb("wlo", [P, UNITS, 4, 256], F32R)
        hhi = sb("hhi", [P, KT, S], F32R)
        hlo = sb("hlo", [P, KT, S], F32R)
        ohi = sb("ohi", [P, 16, S], F32R)
        olo = sb("olo", [P, 16, S], F32R)
        x = sb("x", [P, KT, S])
        ring = sb("ada_ring", [P, 2, KT, 128])
        cols = sb("columns", [P, N_COLS])
        cst = sb("cst", [P, N_CONST])
        ones = sb("ones", [P, P])
        epsc = sb("epsc", [P, 2])
        mod = sb("mod", [P, 48])
        gsc = sb("gsc", [P, 16])
        sil = sb("sil", [P, KT])
        ar = sb("arena", [P, 18432])

        ident = cst[:, C_IDENT:C_IDENT + P]
        causal = cst[:, C_CAUSAL:C_CAUSAL + P]
        strict = cst[:, C_STRICT:C_STRICT + P]
        onehot = cst[0:32, C_ONEHOT:C_ONEHOT + S]

        def col(name, k=0):
            return cols[:, COLS[name] + k:COLS[name] + k + 1]

        def A(at, *shape, parts=P):
            n = int(np.prod(shape))
            v = ar[0:parts, at:at + n]
            if len(shape) == 2:
                v = v.rearrange("p (a b) -> p a b", a=shape[0])
            if len(shape) == 3:
                v = v.rearrange("p (a b c) -> p a b c", a=shape[0], b=shape[1])
            return v

        qh, kh, zt = A(0, 8, S), A(2048, 8, S), A(4096, 8, S)
        vb = A(6144, 16, P)
        kdec, kbe = A(8192, 8, P), A(9216, 8, P)
        qkd = A(10240, 16, P)
        nt = A(12288, 16, P)
        tt = A(14336, 16, P)
        uu = A(16384, 16, P)
        hf_a, xsq_a = A(10240, 8, S), A(12288, 8, S)
        pre = A(14336, 6, 259)
        sq_a, rs_a = A(16384, 4, S), A(13312, 4, S)
        vsil = A(17920, 2, S)
        raw_a = A(12288, 4, S)
        st1, vn0, vn1, wt_ = A(12288, 8, P), A(13312, 8, P), A(14336, 8, P), A(2048, 8, P)
        osq, ors, oof = A(15360, 4, S), A(3072, 4, S), A(8192, 2, S)
        pp = ring[:, 0:1, :, :].rearrange("p a b c -> p (a b c)")[:, 0:1024].rearrange("p (a b) -> p a b", a=4)
        ee = ring[:, 1:2, :, :].rearrange("p a b c -> p (a b c)")[:, 0:512].rearrange("p (a b) -> p a b", a=4)
        ke = ring[:, 1:2, :, :].rearrange("p a b c -> p (a b c)")[:, 512:1024].rearrange("p (a b) -> p a b", a=4)
        r16 = sb("r16", [16, 2, S])
        rt16 = A(9216, 4, S, parts=16)
        ada_sum = sb("ada_sum", [P, 6, P])
        lmask = sb("lmask", [P, LEVELS, 256], U8)
        mask_in = A(8704, LEVELS * 64).bitcast(I32)
        hc = sb("hc", [P, 5, 16])

        bias_at = 0
        hf, xsq = A(6144, 8, S), A(8192, 8, S)
        qraw, kraw = A(10240, 2, S), A(10752, 2, S)
        qn, kn = A(11264, 2, S), A(11776, 2, S)
        sqb, rsb = A(12288, 4, S), A(13312, 4, S)
        zs = A(14336, 4, S)
        vs = A(15360, 2, 512)
        ts = A(16384, 2, 384)
        pt = A(17152, 2, 384)
        of = A(8192, 2, S)
        sm = A(17920, 4, 4)
        cost, sint = A(0, S), A(256, S)
        dmat = A(512, 4, 384)
        rt1, rt2 = A(16384, 2, S), A(16896, 2, S)
        sd = A(17408, 384)
        posi = A(2048, S).bitcast(I32)
        ang = A(2304, S)
        tr1, tr2 = A(2560, S), A(2816, S)
        sq4 = A(2048, 4, S)
        zs_c = A(6144, 8, S)
        fb = sb("fb", [16, 512])
        rcol = sb("rcol", [16, 1])

        ps = [ctx.enter_context(nc.psum_tensor(f"ps{i}", [P, 512], F32)) for i in range(8)]
        pj = [ps[0], ps[1]]
        ssb = ps[2]

        def v2(b, w=S):
            return b[:, :].rearrange("p (a b) -> p a b", b=w)

        def turned_bank(hh, soft0):
            return ps[(7 if soft0 else 2) if hh else 5][:, 0:3 * P]

        def group_banks(g):
            return (ps[0], ps[1], ps[7], ps[2]) if g % 2 else (ps[3], ps[4], ps[5], ps[6])

        x_in_sem = sem("x_in")
        cols_in_sem = sem("cols_in")
        const_in_sem = sem("const_in")
        ab_in_sem = sem("ab_in")
        rel_in_sem = sem("rel_in")
        rel_d_in_sem = sem("rel_d_in")
        lmask_in_sem = sem("lmask_in")
        pos_in_sem = sem("pos_in")
        dtab_in_sem = sem("dtab_in")
        ones_ok_sem = sem("ones_ok")
        w_units_sem = sem("w_units")
        hi_ok_sem = sem("hi_ok")
        lo_ok_sem = sem("lo_ok")
        sq_ok_sem = sem("sq_ok")
        ss_ok_sem = sem("ss_ok")
        ss_read_sem = sem("ss_read")
        rs_ok_sem = sem("rs_ok")
        hf_ok_sem = sem("hf_ok")
        hh_ok_sem = sem("hh_ok")
        h_ok_sem = sem("h_ok")
        dve_own_sem = sem("dve_own")
        ab_ok_sem = sem("ab_ok")
        rows_ok_sem = sem("rows_ok")
        scan_ok_sem = sem("scan_ok")
        rowsT_ok_sem = sem("rowsT_ok")
        bcol_ok_sem = sem("bcol_ok")
        conv_ok_sem = sem("conv_ok")
        qk_raw_sem = sem("qk_raw")
        qk_sq_sem = sem("qk_sq")
        qk_ok_sem = sem("qk_ok")
        vsil_ok_sem = sem("vsil_ok")
        vT_ok_sem = sem("vT_ok")
        vb_ok_sem = sem("vb_ok")
        delta_in_sem = sem("delta_in")
        gl_ok_sem = sem("gl_ok")
        e_pre_sem = sem("e_pre")
        e_ok_sem = sem("e_ok")
        nt_ok_sem = sem("nt_ok")
        kT_ok_sem = sem("kT_ok")
        kcol_ok_sem = sem("kcol_ok")
        p_ok_sem = sem("p_ok")
        pe_v_sem = sem("pe_v")
        tp_ok_sem = sem("tp_ok")
        t_ok_sem = sem("t_ok")
        ut_ok_sem = sem("ut_ok")
        u_ok_sem = sem("u_ok")
        un_ok_sem = sem("un_ok")
        vn_ok_sem = sem("vn_ok")
        st_ok_sem = sem("st_ok")
        stv_sem = sem("stv")
        wt_ok_sem = sem("wt_ok")
        wv_sem = sem("wv")
        vn1_ok_sem = sem("vn1_ok")
        vn1v_sem = sem("vn1v")
        o_ok_sem = sem("o_ok")
        o_sq_sem = sem("o_sq")
        egb_sem = sem("egb")
        o_split_sem = sem("o_split")
        sil_ok_sem = sem("sil_ok")
        ada_used_sem = sem("ada_used")
        ada_mul_sem = sem("ada_mul")
        ada_step_sem = sem("ada_step")
        mod_ok_sem = sem("mod_ok")
        sc_ok_sem = sem("sc_ok")
        m_ok_sem = sem("m_ok")
        mask_ok_sem = sem("mask_ok")
        bias_ps_sem = sem("bias_ps")
        bias_sb_sem = sem("bias_sb")
        scr_out_sem = sem("scr_out")
        bias_ok_sem = sem("bias_ok")
        s_ok_sem = sem("s_ok")
        t_soft_sem = sem("t_soft")
        e_soft_sem = sem("e_soft")
        p_soft_sem = sem("p_soft")
        pT_ok_sem = sem("pT_ok")
        pT_v_sem = sem("pT_v")
        fin_rope_sem = sem("fin_rope")
        rope_ok_sem = sem("rope_ok")
        sd_ok_sem = sem("sd_ok")
        out_ok_sem = sem("out_ok")
        xn_ok_sem = sem("xn_ok")
        ce_sem = sem("ce")
        boot_sem = sem("boot")
        tt_ok_sem = sem("tt_ok")
        rowsv_sem = sem("rowsv")
        raw_in = [sem(f"raw_in{i}") for i in range(RAW)]
        ada_in = [sem(f"ada_in{i}") for i in range(2)]
        bank_free = [sem(f"bank_free{i}") for i in range(2)]
        block = ctx.enter_context(nc.Block())

        @block.sync
        def _(sp):
            sp.dma_start(x[:, 0:4, :], x_in[:, 0:4, :]).then_inc(x_in_sem, 16)
            sp.dma_start(x[:, 4:8, :], x_in[:, 4:8, :]).then_inc(x_in_sem, 16)
            sp.dma_start(cols[:, :], cols_in).then_inc(cols_in_sem, 16)
            for c in range(N_CHUNKS):
                if c >= RAW:
                    sp.wait_ge(lo_ok_sem, max(2 * (c - RAW) + 2, 0))
                sp.dma_start(raw[:, c % RAW, :, :].rearrange("p a b -> p (a b)"), wts[c]).then_inc(raw_in[c % RAW], 16)
                if c == 0:
                    sp.dma_start(cst[:, :], const_in).then_inc(const_in_sem, 16)
                    sp.dma_start(A(6144, 8, 16), w_ab).then_inc(ab_in_sem, 16)
                    sp.dma_start(mask_in, lmask_in).then_inc(lmask_in_sem, 16)
                    sp.dma_start(A(8192, 8, parts=32), rel_b).then_inc(rel_in_sem, 16)
                for u in range(ADA_UNITS):
                    if c == (JOB_B + 1 + u if u < 18 else JOB_C + (u - 18) if u < 42 else 76 + 2 * (u - 42)):
                        if u < 2:
                            sp.wait_ge(o_split_sem, 4)
                        else:
                            sp.wait_ge(ada_mul_sem, u - 1)
                        sp.dma_start(ring[:, u % 2, :, :].rearrange("p a b -> p (a b)"), ada_w[u]).then_inc(ada_in[u % 2], 16)
                if c == JOB_C:
                    sp.wait_ge(t_soft_sem, 8)
                    sp.dma_start(posi[:, :], pos.partition_broadcast(P)).then_inc(pos_in_sem, 16)
                    sp.dma_start(dmat[:, :, :], dtab).then_inc(dtab_in_sem, 16)
            for b in range(2):
                sp.wait_ge(bank_free[b], N_JOBS // 2)
            sp.dma_start(out, x[:, :, :]).then_inc(out_ok_sem, 16)
            sp.wait_ge(out_ok_sem, 16)

        @block.gpsimd
        def _(pool):
            pool.memset(ones[:, :], 1.0).then_inc(ones_ok_sem, 1)
            pool.memset(epsc[:, 0:1], EPS).then_inc(ones_ok_sem, 1)
            pool.memset(epsc[:, 1:2], 1.0).then_inc(ones_ok_sem, 1)
            pool.memset(pre[:, :, 0:3], 0.0).then_inc(ones_ok_sem, 1)
            pool.memset(fb[0:8, 256:512], NEG).then_inc(ones_ok_sem, 1)
            pool.memset(rt16[:, 3, :], 1.0).then_inc(ones_ok_sem, 1)
            pool.wait_ge(lmask_in_sem, 16)
            for lv in range(LEVELS):
                pool.tensor_copy(lmask[:, lv, :].rearrange("p (a b) -> p a b", a=4),
                                 mask_in[:, 64 * lv:64 * lv + 64].unsqueeze(1).to_broadcast([P, 4, 64])).then_inc(mask_ok_sem, 1)

            pool.wait_ge(const_in_sem, 16)
            pool.wait_ge(conv_ok_sem, 24)
            pool.tensor_copy(tt[:, :, :], ident.unsqueeze(1).to_broadcast([P, 16, P])).then_inc(tt_ok_sem, 1)

            def ada_unit(u):
                b = ring[:, u % 2, :, :]
                pool.wait_ge(ada_in[u % 2], 16 * (u // 2 + 1))
                pool.tensor_tensor(b, b, sil[:, :].unsqueeze(2).to_broadcast([P, KT, P]), ALU.mult).then_inc(ada_step_sem, 1)
                pool.wait_ge(ada_step_sem, 3 * u + 1)
                pool.tensor_tensor(b[:, 0:4, :], b[:, 0:4, :], b[:, 4:8, :], ALU.add).then_inc(ada_step_sem, 1)
                pool.wait_ge(ada_step_sem, 3 * u + 2)
                pool.tensor_tensor(b[:, 0:2, :], b[:, 0:2, :], b[:, 2:4, :], ALU.add).then_inc(ada_step_sem, 1)
                pool.wait_ge(ada_step_sem, 3 * u + 3)
                if u >= 6:
                    pool.wait_ge(ada_used_sem, u - 5)
                pool.tensor_tensor(ada_sum[:, u % 6, :], b[:, 0, :], b[:, 1, :], ALU.add).then_inc(ada_mul_sem, 1)

            pool.wait_ge(bias_sb_sem, 1)
            pool.dma_start(scr_b.rearrange("p h t -> h p t"), fb[0:8, :].unsqueeze(1).to_broadcast([8, P, 512])).then_inc(scr_out_sem, 16)
            pool.wait_ge(scr_out_sem, 16)
            pool.wait_ge(o_split_sem, 4)
            bias_b = A(bias_at, 8, 384)
            pool.dma_start(bias_b[:, :, 0:256], bass.AP(scr_b.tensor, 127, [[8 * 512 - 1, P], [512, 8], [1, 256]])).then_inc(bias_ok_sem, 16)
            pool.dma_start(bias_b[:, :, 256:384], bass.AP(scr_b.tensor, 255, [[8 * 512 - 1, P], [512, 8], [1, 128]])).then_inc(bias_ok_sem, 16)
            pool.wait_ge(sil_ok_sem, 1)
            for u in range(18):
                ada_unit(u)
            pool.wait_ge(bias_sb_sem, 1)
            pool.dma_start(fb[:, 127:384], rel_d).then_inc(rel_d_in_sem, 16)
            pool.wait_ge(rel_d_in_sem, 16)
            pool.tensor_scalar(fb[:, 0:127], fb[:, 127:254], 0.0, fb[:, 127:128], ALU.mult, ALU.add).then_inc(boot_sem, 1)
            pool.tensor_scalar(fb[:, 384:512], fb[:, 255:383], 0.0, fb[:, 383:384], ALU.mult, ALU.add).then_inc(boot_sem, 1)
            pool.wait_ge(boot_sem, 2)
            pool.dma_start(scr_d.rearrange("p h t -> h p t"), fb[:, :].unsqueeze(1).to_broadcast([16, P, 512])).then_inc(scr_out_sem, 16)
            pool.wait_ge(scr_out_sem, 32)
            for u in range(18, 42):
                ada_unit(u)
            pool.wait_ge(o_split_sem, 12)
            bias_d = A(bias_at, 16, 384)
            for h0 in range(0, 16, 8):
                pool.dma_start(bias_d[:, h0:h0 + 8, 0:256], bass.AP(scr_d.tensor, 127 + 512 * h0, [[16 * 512 - 1, P], [512, 8], [1, 256]])).then_inc(bias_ok_sem, 16)
                pool.dma_start(bias_d[:, h0:h0 + 8, 256:384], bass.AP(scr_d.tensor, 255 + 512 * h0, [[16 * 512 - 1, P], [512, 8], [1, 128]])).then_inc(bias_ok_sem, 16)
            pool.wait_ge(bias_ok_sem, 32 + 64)
            pool.memset(bias_d[0:64, :, 192:256], NEG).then_inc(boot_sem, 1)
            pool.memset(bias_d[0:64, :, 320:384], NEG).then_inc(boot_sem, 1)
            for u in range(42, ADA_UNITS):
                ada_unit(u)

        @block.tensor
        def _(pe):
            own_ss = [0]

            def mm(o, l, r, start, stop, skip=True):
                return pe.matmul(o, l, r, start=start, stop=stop, skip_group_check=skip)

            def job(J, form, hi, lo, ready=None):
                bank = v2(pj[J % 2])
                pe.wait_ge(bank_free[J % 2], J // 2)
                cs = chunks_of(J)
                for n, c in enumerate(cs):
                    for half in range(2):
                        unit = 2 * c + half
                        pe.wait_ge(lo_ok_sem, unit + 1)
                        for kk in range(4):
                            k = 4 * half + kk
                            kx = 8 * n + k
                            if ready is not None and k % 2 == 0 and n == 0:
                                pe.wait_ge(h_ok_sem, ready + k // 2 + 1)
                            for t in range(2):
                                w = slice(t * P, t * P + P)
                                for a, (ws, hs) in enumerate(((whi, hi), (whi, lo), (wlo, hi))):
                                    first = n == 0 and k == 0 and t == 0 and a == 0
                                    last = n == len(cs) - 1 and k == KT - 1 and a == 2
                                    if form == "T":
                                        m = mm(bank[:, t, :], ws[:, unit % UNITS, kk, w], hs[:, kx, :], first, last)
                                    else:
                                        m = mm(bank[:, t, :], hs[:, kx, w], ws[:, unit % UNITS, kk, :], first, last)
                        m.then_inc(w_units_sem, 1)

            def sums(src, n, width, cnt_sem, cnt):
                pe.wait_ge(ss_read_sem, own_ss[0])
                for t in range(n):
                    if cnt_sem is not None:
                        pe.wait_ge(cnt_sem, cnt(t))
                    m = mm(ssb[:, 0:width], ones[:, :], src(t), t == 0, t == n - 1)
                m.then_inc(ss_ok_sem, 1)
                own_ss[0] += 1

            def ada(u):
                if u % 6 == 0:
                    pe.wait_ge(mod_ok_sem, u // 6)
                pe.wait_ge(ada_mul_sem, u + 1)
                mm(ps[7][:, u % 6:u % 6 + 1], ada_sum[:, u % 6, :], ones[:, 0:1], True, True).then_inc(ada_used_sem, 1)

            pe.wait_ge(ones_ok_sem, 6)
            sums(lambda t: xsq_a[:, t, :], 8, S, sq_ok_sem, lambda t: t // 2 + 1)
            pe.wait_ge(const_in_sem, 16)

            def turn_values(i):
                pe.wait_ge(vsil_ok_sem, i + 1)
                pe.wait_ge(vb_ok_sem, i)
                for n in range(4):
                    m = pe.transpose(ps[3][:, n * P:n * P + P], vsil[:, n // 2, (n % 2) * P:(n % 2) * P + P], ident)
                m.then_inc(vT_ok_sem, 1)

            def key_sums(i):
                sums(lambda t: sq_a[:, 2:4, :], 1, 512, qk_sq_sem, lambda t: 2 * i + 2)

            for i in range(4):
                job(3 * i, "T", hhi, hlo, ready=0 if i == 0 else None)
                if i:
                    key_sums(i - 1)
                if i == 1:
                    pe.wait_ge(scan_ok_sem, 1)
                    for c in range(2):
                        for r in range(2):
                            m = pe.transpose(ps[5][:, c * 32 + 16 * r:c * 32 + 16 * r + 16], r16[:, r, c * P:c * P + P], ident[0:16, 0:16])
                    m.then_inc(rowsT_ok_sem, 1)
                if i:
                    turn_values(i - 1)
                job(3 * i + 1, "T", hhi, hlo)
                if i == 0:
                    pe.wait_ge(ab_in_sem, 16)
                    for k in range(KT):
                        m = mm(ps[3][0:16, 0:S], A(6144, 8, 16)[:, k, :], hf_a[:, k, :], k == 0, k == KT - 1)
                    m.then_inc(ab_ok_sem, 1)
                    pe.wait_ge(rel_in_sem, 16)
                    mm(ps[4][0:8, 0:S], A(8192, 8, parts=32), onehot, True, True).then_inc(bias_ps_sem, 1)
                job(3 * i + 2, "T", hhi, hlo)
                sums(lambda t: sq_a[:, 0:2, :], 1, 512, qk_sq_sem, lambda t: 2 * i + 1)
            job(12, "T", hhi, hlo)
            key_sums(3)
            turn_values(3)
            z_step = [0]

            def z_part():
                s = z_step[0]
                z_step[0] += 1
                J, unit, kk = 13 + s // 8, 26 + s // 4, s % 4
                if s % 8 == 0:
                    pe.wait_ge(bank_free[J % 2], J // 2)
                if kk == 0:
                    pe.wait_ge(lo_ok_sem, unit + 1)
                k = s % 8
                for t in range(2):
                    for a, (ws, hs) in enumerate(((whi, hhi), (whi, hlo), (wlo, hhi))):
                        m = mm(v2(pj[J % 2])[:, t, :], ws[:, unit % UNITS, kk, t * P:t * P + P], hs[:, k, :],
                               k == 0 and t == 0 and a == 0, k == KT - 1 and a == 2)
                if kk == 3:
                    m.then_inc(w_units_sem, 1)

            pe.wait_ge(qk_ok_sem, 8)

            def keys_turned(c, b0, b1):
                for h in range(8):
                    m = pe.transpose((b0 if h < 4 else b1)[:, (h % 4) * P:(h % 4) * P + P], kh[:, h, c * P:c * P + P], ident)
                m.then_inc(kT_ok_sem, 1)

            pe.wait_ge(ss_read_sem, own_ss[0])
            keys_turned(1, ps[2], ps[7])
            pe.wait_ge(vb_ok_sem, 4)
            groups = [(0, 0), (0, 4), (1, 0), (1, 4)]
            for g, (c, h0) in enumerate(groups):
                if g == 1:
                    pe.wait_ge(kcol_ok_sem, 1)
                    pe.wait_ge(bank_free[0], 7)
                    pe.wait_ge(bank_free[1], 6)
                if g > 1:
                    pe.wait_ge(nt_ok_sem, max(g - 1, 0))
                sc = slice(c * P, c * P + P)
                gb = group_banks(g)
                for n in range(4):
                    h = h0 + n
                    o = slice(n * P, n * P + P)
                    mm(gb[0][:, o], ident[0:16, h:h + 1].to_broadcast([16, P]), r16[:, 0, sc], True, True)
                    mm(gb[1][:, o], ident[0:16, 8 + h:9 + h].to_broadcast([16, P]), r16[:, 1, sc], True, True)
                    mm(gb[2][:, o], kh[:, h, sc], kh[:, h, sc], True, True)
                    m = mm(gb[3][:, o], kh[:, h, sc], qh[:, h, sc], True, True)
                m.then_inc(delta_in_sem, 1)
            pe.wait_ge(nt_ok_sem, 3)
            keys_turned(0, ps[5], ps[6])
            pe.wait_ge(nt_ok_sem, 4)
            for _ in range(3):
                z_part()
            pe.wait_ge(kcol_ok_sem, 2)
            for lv in range(LEVELS):
                n = 1 << lv
                for g in range(4):
                    b = ps[2 + g]
                    if lv:
                        pe.wait_ge(t_ok_sem, max(4 * (lv - 1) + g + 1, 0))
                    for m4 in range(4):
                        blk = 4 * g + m4
                        T = tt[:, blk, :].rearrange("p (a two b) -> p a two b", two=2, b=n)[:, :, 0, :]
                        m = mm(b[:, m4 * 64:m4 * 64 + 64], nt[:, blk, :], T if lv else ident.rearrange("p (a two) -> p a two", two=2)[:, :, 0], m4 == 0, True)
                    m.then_inc(p_ok_sem, 1)
                z_part()
                for g in range(4):
                    b = ps[2 + g]
                    if lv:
                        pe.wait_ge(u_ok_sem, max(4 * (lv - 1) + g + 1, 0))
                    pe.wait_ge(pe_v_sem, 4 * lv + g + 1)
                    for m4 in range(4):
                        m = mm(b[:, 256 + m4 * 64:256 + m4 * 64 + 64], uu[:, 4 * g + m4, :] if lv else ident, pp[:, g, m4 * 64:m4 * 64 + 64], m4 == 0, True)
                    m.then_inc(tp_ok_sem, 1)
                z_part()
                for g in range(4):
                    b = ps[6 + g % 2]
                    k = 4 * lv + g
                    pe.wait_ge(t_ok_sem, k + 1)
                    pe.wait_ge(u_ok_sem, max(k - 1, 0))
                    for m4 in range(4):
                        m = pe.transpose(b[:, m4 * P:m4 * P + P], tt[:, 4 * g + m4, :], ident)
                    m.then_inc(ut_ok_sem, 1)
                z_part()
            pe.wait_ge(u_ok_sem, 28)
            for g in range(2):
                for n in range(4):
                    h = 4 * g + n
                    m = mm(ps[2 + g][:, n * P:n * P + P], uu[:, h, :], vb[:, h, :], True, True)
                m.then_inc(un_ok_sem, 1)
            for g in range(2):
                for n in range(4):
                    h = 4 * g + n
                    m = mm(ps[4 + g][:, n * P:n * P + P], kbe[:, h, :], uu[:, 8 + h, :], True, True)
                m.then_inc(wt_ok_sem, 1)
            for g in range(2):
                pe.wait_ge(vn_ok_sem, g + 1)
                for n in range(4):
                    h = 4 * g + n
                    m = mm(ps[6 + g][:, n * P:n * P + P], kdec[:, h, :], vn0[:, h, :], True, True)
                m.then_inc(st_ok_sem, 1)
            for g in range(2):
                pe.wait_ge(stv_sem, g + 1)
                pe.wait_ge(wv_sem, g + 1)
                for n in range(4):
                    h = 4 * g + n
                    mm(ps[2 + g][:, n * P:n * P + P], uu[:, 8 + h, :], vb[:, 8 + h, :], n == 0, False)
                    m = mm(ps[2 + g][:, n * P:n * P + P], wt_[:, h, :], st1[:, h, :], False, n == 3)
                m.then_inc(vn1_ok_sem, 1)
            pe.wait_ge(egb_sem, 2)
            for i in range(4):
                b = ps[4 + i % 2]
                pe.wait_ge(vn1v_sem, i // 2 + 1)
                pe.wait_ge(o_split_sem, max(i - 1, 0))
                for n in range(2):
                    h = 2 * i + n
                    mm(b[:, n * S:n * S + P], vn0[:, h, :], qkd[:, h, :], n == 0, False)
                    mm(b[:, n * S + P:n * S + S], st1[:, h, :], qh[:, h, P:S], False, False)
                    m = mm(b[:, n * S + P:n * S + S], vn1[:, h, :], qkd[:, 8 + h, :], False, n == 1)
                m.then_inc(o_ok_sem, 1)
                sums(lambda t: osq[:, 2 * (i % 2):2 * (i % 2) + 2, :], 1, 512, o_sq_sem, lambda t: i + 1)
            pe.wait_ge(o_split_sem, 4)
            for J in range(JOB_OUT_A, JOB_B):
                job(J, "T", ohi, olo)

            def x_sums(n):
                sums(lambda t: xsq[:, t, :], 8, S, sq_ok_sem, lambda t: 4 * n + t // 2 + 1)

            def attend(J0, pairs, soft0, o0, h_q, h_kv, normed, ready, extra):
                def turn(i):
                    pe.wait_ge(p_soft_sem, soft0 + i + 1)
                    if soft0 == 0:
                        pe.wait_ge(ss_read_sem, own_ss[0])
                    for hh in range(2):
                        if soft0 == 4 and i == 5:
                            pe.wait_ge(mod_ok_sem, 8)
                        if soft0 + i:
                            pe.wait_ge(pT_v_sem, 2 * (soft0 + i) - 1 + hh)
                        for a, c0 in enumerate((256, 0, 128)):
                            m = pe.transpose(turned_bank(hh, soft0)[:, a * P:a * P + P], ts[:, hh, c0:c0 + P], ident)
                        m.then_inc(pT_ok_sem, 1)

                def mix(i):
                    pe.wait_ge(pT_v_sem, 2 * (soft0 + i) + 2)
                    Jv = J0 + 4 * i + 3
                    pe.wait_ge(bank_free[Jv % 2], Jv // 2 + 1)
                    pe.wait_ge(o_split_sem, o0 + i)
                    for hh in range(2):
                        mm(ps[6][:, hh * S:hh * S + S], vs[:, 0, hh * P:hh * P + P], pt[:, hh, 0:256], hh == 0, False)
                        m = mm(ps[6][:, hh * S + P:hh * S + S], vs[:, 1, hh * P:hh * P + P], pt[:, hh, 256:384], False, hh == 1)
                    m.then_inc(o_ok_sem, 1)

                for i in range(pairs):
                    J = J0 + 4 * i
                    job(J, "T", *h_q, ready=ready[0] if i == 0 else None)
                    extra(J)
                    job(J + 1, "T", *h_kv, ready=ready[1] if i == 0 else None)
                    extra(J + 1)
                    if i:
                        turn(i - 1)
                    if normed:
                        sums(lambda t: sqb[:, 0:2, :], 1, 512, qk_sq_sem, lambda t: 8 + 2 * i + 1)
                    job(J + 2, "T", *h_q)
                    extra(J + 2)
                    if i:
                        mix(i - 1)
                    if normed:
                        sums(lambda t: sqb[:, 2:4, :], 1, 512, qk_sq_sem, lambda t: 8 + 2 * i + 2)
                    job(J + 3, "S", *h_kv)
                    extra(J + 3)
                    if normed:
                        pe.wait_ge(qk_ok_sem, 8 + 2 * i + 2)
                    else:
                        for b in range(2):
                            pe.wait_ge(bank_free[b], J // 2 + 1)
                    pe.wait_ge(t_soft_sem, 2 * (soft0 + i))
                    for hh in range(2):
                        mm(ps[3 + hh][:, 0:256], qn[:, hh, P:S], kn[:, hh, :], True, False)
                        m = mm(ps[3 + hh][:, 256:384], qn[:, hh, 0:P], kn[:, hh, 0:P], False, True)
                        m.then_inc(s_ok_sem, 1)
                turn(pairs - 1)
                mix(pairs - 1)

            x_sums(1)

            def ada_b(J):
                if J >= 24:
                    ada(J - 24)

            attend(JOB_B, 4, 0, 4, (ohi[:, 8:16, :], olo[:, 8:16, :]), (hhi, hlo), False, (4, 8), ada_b)
            pe.wait_ge(o_split_sem, 8)
            for J in range(JOB_OUT_B, JOB_C):
                job(J, "T", ohi, olo)
                ada(J - 24)
            x_sums(2)
            ada(16)
            ada(17)
            x_sums(3)

            def mix_c(h):
                for Jv in (JOB_C + 6 * h + 4, JOB_C + 6 * h + 5):
                    pe.wait_ge(bank_free[Jv % 2], Jv // 2 + 1)
                pe.wait_ge(sd_ok_sem, h + 1)
                pe.wait_ge(o_split_sem, 8 + h)
                for t in range(4):
                    b = ps[3 + t // 2]
                    c0 = (t % 2) * S
                    mm(b[:, c0:c0 + S], vs[:, 0, t * P:t * P + P], sd[:, 0:256], t % 2 == 0, False)
                    m = mm(b[:, c0 + P:c0 + S], vs[:, 1, t * P:t * P + P], sd[:, 256:384], False, t % 2 == 1)
                m.then_inc(o_ok_sem, 1)

            def sums_c(h):
                sums(lambda t: sq4[:, t, :], 4, S, o_sq_sem, lambda t: 4 + h + 1)

            def ada_c(J):
                if J >= JOB_C + 3:
                    ada(J - 25)

            for h in range(4):
                J = JOB_C + 6 * h
                job(J, "T", hhi, hlo, ready=12 if h == 0 else None)
                ada_c(J)
                if h:
                    mix_c(h - 1)
                job(J + 1, "T", hhi, hlo)
                ada_c(J + 1)
                job(J + 2, "T", hhi, hlo)
                ada_c(J + 2)
                if h:
                    sums_c(h - 1)
                pe.wait_ge(rope_ok_sem, 2 * h + 2)
                pe.wait_ge(sd_ok_sem, h)
                for kt in range(2):
                    mm(ps[5][:, 0:256], kn[:, kt, 0:P], qn[:, kt, :], kt == 0, False)
                    m = mm(ps[5][:, 256:384], kn[:, kt, P:S], qn[:, kt, P:S], False, kt == 1)
                m.then_inc(sc_ok_sem, 1)
                job(J + 3, "T", hhi, hlo)
                ada_c(J + 3)
                job(J + 4, "S", hhi, hlo)
                ada_c(J + 4)
                job(J + 5, "S", hhi, hlo)
                ada_c(J + 5)
            mix_c(3)
            sums_c(3)
            for u in range(39, 42):
                ada(u)
            pe.wait_ge(o_split_sem, 12)
            for J in range(JOB_OUT_C, JOB_D):
                job(J, "T", ohi, olo)
            x_sums(4)

            def ada_d(J):
                if J == 91:
                    pe.wait_ge(pT_v_sem, 18)
                    for u in range(42, ADA_UNITS):
                        ada(u)

            attend(JOB_D, 8, 4, 12, (hhi, hlo), (hhi, hlo), True, (16, 16), ada_d)
            pe.wait_ge(o_split_sem, 20)
            for J in range(JOB_OUT_D, N_JOBS):
                job(J, "T", ohi, olo)

        @block.scalar
        def _(act):
            ss_n = [0]

            def ln_exp_set():
                act.add_instruction(mybir.InstLoadActFuncSet(name=nc.get_next_instruction_name(), act_func_set_id=6, ins=[], outs=[]))

            def high(c):
                if c >= N_CHUNKS:
                    return
                for half in range(2):
                    unit = 2 * c + half
                    act.wait_ge(raw_in[c % RAW], 16 * (c // RAW + 1))
                    act.wait_ge(w_units_sem, max(unit + 1 - UNITS, 0))
                    act.wait_ge(lo_ok_sem, max(unit + 1 - UNITS, 0))
                    act.activation(whi[:, unit % UNITS, :, :], raw[:, c % RAW, 4 * half:4 * half + 4, :], ACT.Copy).then_inc(hi_ok_sem, 1)

            def at_job(J):
                for c in chunks_of(J):
                    high(c + 1)
                act.wait_ge(w_units_sem, 2 * chunks_of(J)[-1] + 2)

            def bank(J):
                return v2(pj[J % 2])

            def bank_taken(e, J):
                e.wait_ge(bank_free[J % 2], J // 2 + 1)

            def rsqrt(dst, width, scale):
                ss_n[0] += 1
                act.wait_ge(ss_ok_sem, ss_n[0])
                act.activation(dst, ssb[:, 0:width] if len(dst.shape) == 2 else v2(ssb), ACT.Ln, scale=scale, bias=epsc[:, 0:1]).then_inc(ss_read_sem, 1)
                act.wait_ge(ss_read_sem, ss_n[0])
                act.activation(dst, dst, ACT.Exp, scale=-0.5).then_inc(rs_ok_sem, 1)

            def split_h(prep, src, dst):
                for t in range(4):
                    act.wait_ge(hf_ok_sem, 8 * prep + 2 * t + 2)
                    act.activation(dst[:, 2 * t:2 * t + 2, :], src[:, 2 * t:2 * t + 2, :], ACT.Copy).then_inc(hh_ok_sem, 1)

            def square_x(J0):
                for n in range(4):
                    J = J0 + n
                    for c in chunks_of(J):
                        high(c + 1)
                    bank_taken(act, J)
                    act.activation(xsq[:, 2 * n:2 * n + 2, :], x[:, 2 * n:2 * n + 2, :], ACT.Square).then_inc(sq_ok_sem, 1)

            act.wait_ge(x_in_sem, 32)
            for t in range(4):
                act.activation(xsq_a[:, 2 * t:2 * t + 2, :], x[:, 2 * t:2 * t + 2, :], ACT.Square).then_inc(sq_ok_sem, 1)
            ln_exp_set()
            act.wait_ge(ones_ok_sem, 6)
            rsqrt(rs_a[:, 0, :], S, 1.0 / D)
            high(0)
            split_h(0, hf_a, hhi)
            act.wait_ge(cols_in_sem, 16)
            act.activation(sil[:, :], cols[:, COLS["cond"]:COLS["cond"] + KT], ACT.Silu).then_inc(sil_ok_sem, 1)

            for i in range(4):
                for k in range(3):
                    J = 3 * i + k
                    at_job(J)
                    act.wait_ge(conv_ok_sem, max(6 * (i - 1) + 2 * k + 2, 0))
                    act.activation(pre[:, 2 * k:2 * k + 2, 3:259], bank(J), ACT.Copy).then_inc(bank_free[J % 2], 1)
                    if k == 0 and i:
                        rsqrt(rs_a[:, 2:4, :], 512, 1.0)
                    if k:
                        r = slice(2 * k - 2, 2 * k)
                        act.wait_ge(conv_ok_sem, 6 * i + 2 * k)
                        act.activation(raw_a[:, r, :], raw_a[:, r, :], ACT.Silu).then_inc(qk_raw_sem, 1)
                        act.wait_ge(qk_raw_sem, 2 * i + k)
                        act.activation(sq_a[:, r, :], raw_a[:, r, :], ACT.Square).then_inc(qk_sq_sem, 1)
                if i == 0:
                    ln_exp_set()
                    act.wait_ge(rows_ok_sem, 1)
                    act.activation(rt16[:, 1, :], rt16[:, 1, :], ACT.Exp, scale=-1.0).then_inc(rowsv_sem, 1)
                    act.activation(rcol[:, :], cols[0:16, COLS["rows"] + 1:COLS["rows"] + 2], ACT.Exp)
                    act.wait_ge(rowsv_sem, 1)
                    act.activation(rt16[:, 1, :], rt16[:, 1, :], ACT.Ln, bias=epsc[0:16, 1:2]).then_inc(rowsv_sem, 1)
                    act.wait_ge(rows_ok_sem, 2)
                    act.activation(r16[:, 1, :], r16[:, 1, :], ACT.Exp).then_inc(scan_ok_sem, 1)
                act.wait_ge(conv_ok_sem, 6 * i + 6)
                act.activation(vsil[:, :, :], vsil[:, :, :], ACT.Silu).then_inc(vsil_ok_sem, 1)
                ln_exp_set()
                rsqrt(rs_a[:, 0:2, :], 512, 1.0)
            at_job(12)
            rsqrt(rs_a[:, 2:4, :], 512, 1.0)
            act.wait_ge(rowsT_ok_sem, 1)
            act.wait_ge(bcol_ok_sem, 1)
            act.activation(hc[:, 2, 8:16], hc[:, 0, 8:16], ACT.Exp).then_inc(ce_sem, 1)
            act.activation(zt[:, 0:2, :], bank(12), ACT.Silu).then_inc(bank_free[0], 1)
            ln_exp_set()
            for g in range(4):
                act.wait_ge(e_pre_sem, g + 1)
                act.activation(ee[:, :, :], ee[:, :, :], ACT.Exp).then_inc(e_ok_sem, 1)
                if g >= 2:
                    act.wait_ge(nt_ok_sem, g)
                    act.activation(pp[:, 0:2, :], v2(group_banks(g)[0]), ACT.Exp).then_inc(egb_sem, 1)
                if g == 1:
                    act.wait_ge(gl_ok_sem, 1)
                    act.activation(hc[:, 2, 0:8], hc[:, 3, 0:8], ACT.Exp).then_inc(ce_sem, 1)
            high(14)

            def gate_z(J):
                i = J - 12
                act.wait_ge(w_units_sem, 2 * J + 2)
                act.activation(zt[:, 2 * i:2 * i + 2, :], bank(J), ACT.Silu).then_inc(bank_free[J % 2], 1)

            for lv in range(LEVELS):
                for g in range(4):
                    act.wait_ge(p_ok_sem, 4 * lv + g + 1)
                    act.activation(pp[:, g, :], ps[2 + g][:, 0:256], ACT.Copy).then_inc(pe_v_sem, 1)
                for g in range(4):
                    act.wait_ge(ut_ok_sem, 4 * lv + g + 1)
                    act.activation(uu[:, 4 * g:4 * g + 4, :], v2(ps[6 + g % 2], P), ACT.Copy).then_inc(u_ok_sem, 1)
                if lv in (1, 4):
                    high(15 + lv // 4)
                    gate_z(13 + lv // 4)
            gate_z(15)
            ln_exp_set()
            for g in range(2):
                act.wait_ge(un_ok_sem, g + 1)
                act.activation(vn0[:, 4 * g:4 * g + 4, :], v2(ps[2 + g], P), ACT.Copy).then_inc(vn_ok_sem, 1)
            for g in range(2):
                act.wait_ge(wt_ok_sem, g + 1)
                act.activation(wt_[:, 4 * g:4 * g + 4, :], v2(ps[4 + g], P), ACT.Copy).then_inc(wv_sem, 1)
            for g in range(2):
                act.wait_ge(vn1_ok_sem, g + 1)
                act.activation(vn1[:, 4 * g:4 * g + 4, :], v2(ps[2 + g], P), ACT.Copy).then_inc(vn1v_sem, 1)
            for i in range(4):
                p2 = slice(2 * (i % 2), 2 * (i % 2) + 2)
                act.wait_ge(o_ok_sem, i + 1)
                act.activation(osq[:, p2, :], v2(ps[4 + i % 2]), ACT.Square).then_inc(o_sq_sem, 1)
                act.wait_ge(o_split_sem, max(i - 1, 0))
                rsqrt(ors[:, p2, :], 512, 1.0 / DH)
            square_x(JOB_OUT_A)

            def attend(J0, pairs, soft0, v0, normed):
                def soft(i):
                    si = soft0 + i
                    for hh in range(2):
                        act.wait_ge(m_ok_sem, 2 * si + hh + 1)
                        for a, (c0, c1) in enumerate(((0, 256), (256, 384))):
                            k = 2 * hh + a
                            m = act.activation(ts[:, hh, c0:c1], ts[:, hh, c0:c1], ACT.Exp, bias=sm[:, 0, k:k + 1], accum_out=sm[:, 1, k:k + 1])
                        m.then_inc(e_soft_sem, 1)

                def turned(i):
                    for hh in range(2):
                        act.wait_ge(pT_ok_sem, 2 * (soft0 + i) + hh + 1)
                        act.activation(pt[:, hh, :], turned_bank(hh, soft0), ACT.Copy).then_inc(pT_v_sem, 1)

                def split_c(J):
                    for c in chunks_of(J):
                        high(c + 1)

                for i in range(pairs):
                    J = J0 + 4 * i
                    split_c(J)
                    if i:
                        if normed:
                            ln_exp_set()
                        soft(i - 1)
                    for k, (raw_, to) in enumerate(((qraw, qn), (kraw, kn))):
                        if k:
                            split_c(J + 1)
                        act.wait_ge(w_units_sem, 2 * chunks_of(J + k)[-1] + 2)
                        if normed:
                            act.activation(sqb[:, 2 * k:2 * k + 2, :], bank(J + k), ACT.Square).then_inc(qk_sq_sem, 1)
                            act.wait_ge(qk_ok_sem, max(8 + 2 * (i - 1) + k + 1, 0))
                            act.activation(raw_[:, :, :], bank(J + k), ACT.Copy).then_inc(bank_free[(J + k) % 2], 1)
                        else:
                            act.wait_ge(s_ok_sem, 2 * (soft0 + i))
                            act.activation(to[:, :, :], bank(J + k), ACT.Copy).then_inc(bank_free[(J + k) % 2], 1)
                    if i:
                        turned(i - 1)
                    if normed:
                        if i == 0:
                            ln_exp_set()
                        rsqrt(rsb[:, 0:2, :], 512, 1.0 / DH)
                    split_c(J + 2)
                    split_c(J + 3)
                    if normed:
                        rsqrt(rsb[:, 2:4, :], 512, 1.0 / DH)
                    act.wait_ge(w_units_sem, 2 * chunks_of(J + 2)[-1] + 2)
                    act.activation(zs[:, 2 * (i % 2):2 * (i % 2) + 2, :], bank(J + 2), ACT.Silu).then_inc(bank_free[J % 2], 1)
                    act.wait_ge(w_units_sem, 2 * chunks_of(J + 3)[-1] + 2)
                    act.wait_ge(o_ok_sem, v0 + i)
                    act.activation(vs[:, :, 0:256], bank(J + 3), ACT.Copy).then_inc(bank_free[(J + 3) % 2], 1)
                ln_exp_set()
                soft(pairs - 1)
                turned(pairs - 1)

            ln_exp_set()
            rsqrt(rsb[:, 0, :], S, 1.0 / D)
            split_h(1, hf, ohi[:, 8:16, :])
            split_h(2, hf, hhi)
            attend(JOB_B, 4, 0, 4, False)
            square_x(JOB_OUT_B)
            ln_exp_set()
            rsqrt(rsb[:, 0, :], S, 1.0 / D)
            for t in range(4):
                act.wait_ge(xn_ok_sem, t + 1)
                act.activation(xsq[:, 2 * t:2 * t + 2, :], x[:, 2 * t:2 * t + 2, :], ACT.Square).then_inc(sq_ok_sem, 1)
            rsqrt(rsb[:, 0, :], S, 1.0 / D)
            split_h(3, hf, hhi)
            act.wait_ge(fin_rope_sem, 1)
            act.activation(sint, tr1, ACT.Sin)
            act.activation(cost, tr2, ACT.Sin).then_inc(fin_rope_sem, 1)
            for h in range(5):
                J = JOB_C + 6 * h
                if h < 4:
                    high(J + 1)
                    high(J + 2)
                if h < 4:
                    high(J + 3)
                if h:
                    act.wait_ge(o_ok_sem, 8 + h)
                    act.activation(sq4[:, 0:2, :], v2(ps[3]), ACT.Square)
                    act.activation(sq4[:, 2:4, :], v2(ps[4]), ACT.Square).then_inc(o_sq_sem, 1)
                if h < 4:
                    act.wait_ge(w_units_sem, 2 * (J + 2) + 2)
                    act.activation(zs_c[:, 4 * (h % 2):4 * (h % 2) + 2, :], bank(J + 2), ACT.Silu).then_inc(bank_free[J % 2], 1)
                    high(J + 4)
                    act.wait_ge(w_units_sem, 2 * (J + 3) + 2)
                    act.activation(zs_c[:, 4 * (h % 2) + 2:4 * (h % 2) + 4, :], bank(J + 3), ACT.Silu).then_inc(bank_free[(J + 1) % 2], 1)
                if h:
                    ln_exp_set()
                    rsqrt(rsb[:, 0, :], S, 1.0 / 512)
                if h < 4:
                    for k in range(2):
                        high(J + 5 + k)
                        act.wait_ge(w_units_sem, 2 * (J + 4 + k) + 2)
                        act.wait_ge(o_ok_sem, 8 + h)
                        act.activation(vs[:, :, 256 * k:256 * k + 256], bank(J + 4 + k), ACT.Copy).then_inc(bank_free[(J + k) % 2], 1)
            square_x(JOB_OUT_C)
            rsqrt(rsb[:, 0, :], S, 1.0 / D)
            split_h(4, hf, hhi)
            attend(JOB_D, 8, 4, 12, True)
            for J in range(JOB_OUT_D, N_JOBS):
                for c in chunks_of(J):
                    high(c + 1)

        @block.vector
        def _(dve):
            steps = [0]

            def own(ins):
                steps[0] += 1
                ins.then_inc(dve_own_sem, 1)

            rs_n = [0]

            def low(c):
                if c >= N_CHUNKS:
                    return
                for half in range(2):
                    unit = 2 * c + half
                    dve.wait_ge(hi_ok_sem, unit + 1)
                    dve.tensor_tensor(wlo[:, unit % UNITS, :, :], raw[:, c % RAW, 4 * half:4 * half + 4, :],
                                      whi[:, unit % UNITS, :, :].bitcast(F32), ALU.subtract).then_inc(lo_ok_sem, 1)

            def lows(J):
                for c in chunks_of(J):
                    low(c + 1)

            def sums_done(J):
                dve.wait_ge(w_units_sem, 2 * chunks_of(J)[-1] + 2)

            def bank(J):
                return v2(pj[J % 2])

            def next_rs():
                rs_n[0] += 1
                dve.wait_ge(rs_ok_sem, rs_n[0])

            def wide(v, n):
                return v.unsqueeze(1).to_broadcast([P, n, v.shape[-1]])

            def prepare(prep, gain, shift, f, rs, hi, lo):
                def lo_part(p):
                    dve.wait_ge(hh_ok_sem, 4 * prep + p + 1)
                    r = slice(2 * p, 2 * p + 2)
                    dve.tensor_tensor(lo[:, r, :], f[:, r, :], hi[:, r, :].bitcast(F32), ALU.subtract).then_inc(h_ok_sem, 1)

                dve.wait_ge(h_ok_sem, 4 * prep)
                for t in range(KT):
                    m = dve.scalar_tensor_tensor(out=f[:, t, :], in0=x[:, t, :], scalar=gain(t), in1=rs, op0=ALU.mult, op1=ALU.mult)
                    if shift is not None:
                        own(m)
                        dve.wait_ge(dve_own_sem, steps[0])
                        m = dve.tensor_scalar(f[:, t, :], f[:, t, :], shift(t), None, ALU.add)
                    m.then_inc(hf_ok_sem, 1)
                    if t >= 3 and t % 2:
                        lo_part(t // 2 - 1)
                lo_part(3)

            def split_o(src, tile, n):
                dve.wait_ge(dve_own_sem, steps[0])
                r = slice(tile, tile + n)
                own(dve.tensor_copy(ohi[:, r, :], src))
                dve.wait_ge(dve_own_sem, steps[0])
                return dve.tensor_tensor(olo[:, r, :], src, ohi[:, r, :].bitcast(F32), ALU.subtract)

            dve.wait_ge(cols_in_sem, 16)
            next_rs()
            low(0)
            prepare(0, lambda t: col("a_norm", t), None, hf_a, rs_a[:, 0, :], hhi, hlo)

            def conv(i, k, dst):
                dve.wait_ge(qk_ok_sem, max(2 * i - 1 if k == 0 else 2 * i, 0))
                for t in range(2):
                    tile = 8 * k + 2 * i + t
                    u = pre[:, 2 * k + t, :]
                    own(dve.tensor_scalar(dst[:, t, :], u[:, 3:259], col("conv", 4 * tile + 3), None, ALU.mult))
                    for j in (2, 1, 0):
                        dve.wait_ge(dve_own_sem, steps[0])
                        m = dve.scalar_tensor_tensor(out=dst[:, t, :], in0=u[:, j:j + S], scalar=col("conv", 4 * tile + j), in1=dst[:, t, :], op0=ALU.mult, op1=ALU.add)
                        if j:
                            own(m)
                    m.then_inc(conv_ok_sem, 1)

            def take_mod(i):
                dve.wait_ge(ada_used_sem, 6 * i + 6)
                a0 = COLS["ada_b"] + 6 * i
                dve.tensor_tensor(mod[:, 6 * i:6 * i + 6], ps[7][:, 0:6], cols[:, a0:a0 + 6], ALU.add).then_inc(mod_ok_sem, 1)

            def take_values(i):
                dve.wait_ge(vT_ok_sem, i + 1)
                for n in range(4):
                    h, c = 2 * i + n // 2, n % 2
                    m = dve.tensor_scalar(vb[:, 8 * c + h, :], ps[3][:, n * P:n * P + P], hc[:, 1, 8 * c + h:8 * c + h + 1], None, ALU.mult)
                m.then_inc(vb_ok_sem, 1)

            def l2_normalised(i, n):
                to, sc = ((qh, DH ** -0.5), (kh, 1.0))[n]
                next_rs()
                dve.scalar_tensor_tensor(out=to[:, 2 * i:2 * i + 2, :], in0=raw_a[:, 2 * n:2 * n + 2, :], scalar=sc, in1=rs_a[:, 2 * n:2 * n + 2, :], op0=ALU.mult, op1=ALU.mult).then_inc(qk_ok_sem, 1)

            dve.wait_ge(ones_ok_sem, 6)
            for i in range(4):
                for k in range(3):
                    J = 3 * i + k
                    lows(J)
                    dve.wait_ge(bank_free[J % 2], J // 2 + 1)
                    if k == 2:
                        dve.wait_ge(vT_ok_sem, i)
                    conv(i, k, raw_a[:, 2 * k:2 * k + 2, :] if k < 2 else vsil)
                    if k == 0 and i:
                        l2_normalised(i - 1, 1)
                    if k == 1 and i == 1:
                        dve.wait_ge(rowsT_ok_sem, 1)
                        for c in range(2):
                            dve.tensor_copy(hc[:, 0, 8 * c:8 * c + 8], ps[5][:, 32 * c:32 * c + 8])
                            m = dve.tensor_copy(hc[:, 1, 8 * c:8 * c + 8], ps[5][:, 32 * c + 24:32 * c + 32])
                        m.then_inc(bcol_ok_sem, 1)
                        dve.wait_ge(bcol_ok_sem, 1)
                    if k == 1 and i:
                        take_values(i - 1)
                    if k == 1 and i == 0:
                        dve.wait_ge(ab_ok_sem, 1)
                        own(dve.tensor_scalar(rt16[:, 0, :], ps[3][0:16, 0:S], cols[0:16, COLS["rows"]:COLS["rows"] + 1], None, ALU.add))
                        dve.wait_ge(dve_own_sem, steps[0])
                        dve.scalar_tensor_tensor(out=rt16[:, 1, :], in0=rt16[:, 0, :], scalar=-1.0, in1=rt16[:, 0, :], op0=ALU.mult, op1=ALU.max).then_inc(rows_ok_sem, 1)
                        dve.wait_ge(bias_ps_sem, 1)
                        dve.tensor_copy(fb[0:8, 0:S], ps[4][0:8, 0:S]).then_inc(bias_sb_sem, 1)
                if i == 0:
                    dve.wait_ge(rowsv_sem, 2)
                    own(dve.scalar_tensor_tensor(out=rt16[:, 2, :], in0=rt16[:, 0, :], scalar=0.0, in1=rt16[:, 1, :], op0=ALU.max, op1=ALU.add))
                    dve.wait_ge(dve_own_sem, steps[0])
                    dve.tensor_tensor(r16[:, 1, :], rt16[:, 0, :], rt16[:, 2, :], ALU.subtract)
                    own(dve.tensor_scalar(rt16[:, 1, :], rt16[:, 2, :], rcol[:, 0:1], -1.0, ALU.mult, ALU.mult))
                    dve.wait_ge(dve_own_sem, steps[0])
                    for c in range(2):
                        cs = slice(c * P, c * P + P)
                        m = dve.tensor_tensor_scan(r16[:, 0, cs], rt16[:, 3, cs], rt16[:, 1, cs], 0.0, ALU.mult, ALU.add)
                    m.then_inc(rows_ok_sem, 1)
                l2_normalised(i, 0)
            lows(12)
            l2_normalised(3, 1)
            take_values(3)

            def keys_by_position(c, to, w, b0, b1):
                dve.wait_ge(kT_ok_sem, 2 - c)
                for h in range(8):
                    m = dve.tensor_scalar(to[:, h, :], (b0 if h < 4 else b1)[:, (h % 4) * P:(h % 4) * P + P], w[:, h:h + 1], None, ALU.mult)
                m.then_inc(kcol_ok_sem, 1)

            dve.wait_ge(mask_ok_sem, LEVELS)
            dve.wait_ge(ce_sem, 1)
            own(dve.scalar_tensor_tensor(out=hc[:, 4, 8:16], in0=hc[:, 1, 8:16], scalar=-1.0, in1=hc[:, 2, 8:16], op0=ALU.mult, op1=ALU.mult))
            dve.wait_ge(dve_own_sem, steps[0])
            keys_by_position(1, kbe, hc[:, 4, 8:16], ps[2], ps[7])
            groups = [(0, 0), (0, 4), (1, 0), (1, 4)]
            for g, (c, h0) in enumerate(groups):
                gb = group_banks(g)
                dve.wait_ge(delta_in_sem, g + 1)
                dve.wait_ge(nt_ok_sem, g)
                for n in range(4):
                    h = h0 + n
                    m = dve.scalar_tensor_tensor(out=ee[:, n, :], in0=gb[0][:, n * P:n * P + P], scalar=hc[:, 0, 8 * c + h:8 * c + h + 1], in1=causal, op0=ALU.subtract, op1=ALU.add)
                m.then_inc(e_pre_sem, 1)
                b4 = slice(4 * g, 4 * g + 4)
                if c == 0:
                    own(dve.tensor_copy(hc[:, 3, h0:h0 + 4], v2(gb[0], P)[:, :, P - 1]))
                    if g == 1:
                        dve.wait_ge(dve_own_sem, steps[0])
                        dve.tensor_tensor(hc[:, 3, 0:8], hc[:, 3, 0:8], hc[:, 0, 0:8], ALU.subtract).then_inc(gl_ok_sem, 1)
                own(dve.tensor_tensor(nt[:, b4, :], v2(gb[1], P), wide(strict, 4), ALU.mult))
                dve.wait_ge(e_ok_sem, g + 1)
                own(dve.tensor_tensor(ke[:, :, :], v2(gb[2], P), ee[:, :, :], ALU.mult))
                own(dve.tensor_tensor(qkd[:, b4, :], v2(gb[3], P), ee[:, :, :], ALU.mult))
                dve.wait_ge(dve_own_sem, steps[0])
                if c == 1:
                    dve.wait_ge(egb_sem, max(g - 1, 0))
                    dve.tensor_tensor(qh[:, h0:h0 + 4, P:S], qh[:, h0:h0 + 4, P:S], pp[:, 0:2, :].rearrange("p a (b c) -> p (a b) c", b=2), ALU.mult)
                dve.tensor_tensor(nt[:, b4, :], nt[:, b4, :], ke[:, :, :], ALU.mult).then_inc(nt_ok_sem, 1)
            dve.wait_ge(ce_sem, 2)
            keys_by_position(0, kdec, hc[:, 2, 0:8], ps[5], ps[6])
            low(14)
            dve.wait_ge(tt_ok_sem, 1)
            for lv in range(LEVELS):
                n = 1 << lv
                if lv in (2, 5):
                    low(15 + lv // 5)
                for g in range(4):
                    dve.wait_ge(tp_ok_sem, 4 * lv + g + 1)
                    T = tt[:, 4 * g:4 * g + 4, :].rearrange("p g c -> p (g c)").rearrange("p (a two b) -> p a two b", two=2, b=n)[:, :, 0, :]
                    dve.copy_predicated(T, lmask[:, lv, :].rearrange("p (a b) -> p a b", b=n), ps[2 + g][:, 256:512].rearrange("p (a b) -> p a b", b=n)).then_inc(t_ok_sem, 1)
            for g in range(2):
                dve.wait_ge(st_ok_sem, g + 1)
                dve.tensor_copy(st1[:, 4 * g:4 * g + 4, :], v2(ps[6 + g], P)).then_inc(stv_sem, 1)
            for i in range(4):
                p2 = slice(2 * (i % 2), 2 * (i % 2) + 2)
                next_rs()
                dve.wait_ge(o_split_sem, i)
                own(dve.scalar_tensor_tensor(out=oof[:, :, :], in0=v2(ps[4 + i % 2]), scalar=col("a_out"), in1=ors[:, p2, :], op0=ALU.mult, op1=ALU.mult))
                dve.wait_ge(dve_own_sem, steps[0])
                own(dve.tensor_tensor(oof[:, :, :], oof[:, :, :], zt[:, 2 * i:2 * i + 2, :], ALU.mult))
                split_o(oof[:, :, :], 2 * i, 2).then_inc(o_split_sem, 1)

            def add_x(J0, gate=None):
                for n in range(4):
                    J = J0 + n
                    lows(J)
                    sums_done(J)
                    if gate is None:
                        dve.tensor_tensor(x[:, 2 * n:2 * n + 2, :], bank(J), x[:, 2 * n:2 * n + 2, :], ALU.add).then_inc(bank_free[J % 2], 1)
                    else:
                        for t in range(2):
                            k = 2 * n + t
                            m = dve.scalar_tensor_tensor(out=x[:, k, :], in0=bank(J)[:, t, :], scalar=mod[:, gate + k:gate + k + 1], in1=x[:, k, :], op0=ALU.mult, op1=ALU.add)
                        m.then_inc(bank_free[J % 2], 1)

            def attend(J0, pairs, soft0, bias, normed, modded):
                def scores_in(i):
                    si = soft0 + i
                    for hh in range(2):
                        dve.wait_ge(s_ok_sem, 2 * si + hh + 1)
                        dve.wait_ge(pT_ok_sem, max(2 * si + hh - 1, 0))
                        own_ts = dve.scalar_tensor_tensor(out=ts[:, hh, :], in0=ps[3 + hh][:, 0:384], scalar=DH ** -0.5, in1=bias[:, 2 * i + hh, :], op0=ALU.mult, op1=ALU.add)
                        own_ts.then_inc(t_soft_sem, 1)
                        dve.wait_ge(t_soft_sem, 2 * si + hh + 1)
                        for a, (c0, c1) in enumerate(((0, 256), (256, 384))):
                            m = dve.tensor_reduce(sm[:, 0, 2 * hh + a:2 * hh + a + 1], ts[:, hh, c0:c1], AX.X, ALU.max, negate=True)
                        m.then_inc(m_ok_sem, 1)

                def scale_p(i):
                    for hh in range(2):
                        dve.wait_ge(e_soft_sem, 2 * (soft0 + i) + hh + 1)
                        dve.wait_ge(p_soft_sem, soft0 + i)
                        own(dve.reciprocal(sm[:, 2, 2 * hh:2 * hh + 2], sm[:, 1, 2 * hh:2 * hh + 2]))
                        dve.wait_ge(dve_own_sem, steps[0])
                        for a, (c0, c1) in enumerate(((0, 256), (256, 384))):
                            m = dve.tensor_scalar(ts[:, hh, c0:c1], ts[:, hh, c0:c1], sm[:, 2, 2 * hh + a:2 * hh + a + 1], None, ALU.mult)
                    m.then_inc(p_soft_sem, 1)

                def finish(i):
                    dve.wait_ge(o_ok_sem, soft_o + i + 1)
                    dve.wait_ge(o_split_sem, soft_o + i)
                    dve.wait_ge(bank_free[J0 % 2], (J0 + 4 * i + 2) // 2 + 1)
                    own(dve.tensor_tensor(of[:, :, :], v2(ps[6]), zs[:, 2 * (i % 2):2 * (i % 2) + 2, :], ALU.mult))
                    split_o(of[:, :, :], 2 * i, 2).then_inc(o_split_sem, 1)

                soft_o = 4 if not normed else 12
                for i in range(pairs):
                    J = J0 + 4 * i
                    lows(J)
                    if i:
                        scores_in(i - 1)
                        scale_p(i - 1)
                    lows(J + 1)
                    if not normed and i == 2:
                        take_mod(0)
                    lows(J + 2)
                    if normed:
                        next_rs()
                        dve.wait_ge(s_ok_sem, 2 * (soft0 + i))
                        dve.scalar_tensor_tensor(out=qn[:, :, :], in0=qraw[:, :, :], scalar=col("att_q"), in1=rsb[:, 0:2, :], op0=ALU.mult, op1=ALU.mult).then_inc(qk_ok_sem, 1)
                    lows(J + 3)
                    if normed:
                        next_rs()
                        dve.scalar_tensor_tensor(out=kn[:, :, :], in0=kraw[:, :, :], scalar=col("att_k"), in1=rsb[:, 2:4, :], op0=ALU.mult, op1=ALU.mult).then_inc(qk_ok_sem, 1)
                    if i:
                        finish(i - 1)
                    if i in modded:
                        take_mod(modded[i])
                scores_in(pairs - 1)
                scale_p(pairs - 1)
                finish(pairs - 1)

            add_x(JOB_OUT_A)
            next_rs()
            prepare(1, lambda t: col("b_norm", t), None, hf, rsb[:, 0, :], ohi[:, 8:16, :], olo[:, 8:16, :])
            prepare(2, lambda t: col("kv_norm", t), None, hf, rsb[:, 0, :], hhi, hlo)
            dve.wait_ge(bias_ok_sem, 32)
            attend(JOB_B, 4, 0, A(bias_at, 8, 384), False, {3: 1})
            add_x(JOB_OUT_B)
            next_rs()
            for t in range(KT):
                m = dve.scalar_tensor_tensor(out=x[:, t, :], in0=x[:, t, :], scalar=col("final_norm", t), in1=rsb[:, 0, :], op0=ALU.mult, op1=ALU.mult)
                if t % 2:
                    m.then_inc(xn_ok_sem, 1)
            take_mod(2)
            dve.wait_ge(mod_ok_sem, 3)
            def scaled_gain(l):
                own(dve.scalar_tensor_tensor(out=gsc[:, 8 * l:8 * l + 8], in0=mod[:, 24 * l + 8:24 * l + 16], scalar=1.0, in1=cols[:, COLS["norm2"] + 8 * l:COLS["norm2"] + 8 * l + 8], op0=ALU.add, op1=ALU.mult))
            scaled_gain(0)
            dve.wait_ge(dve_own_sem, steps[0])
            dve.wait_ge(pos_in_sem, 16)
            own(dve.tensor_copy(ang, posi))
            dve.wait_ge(dve_own_sem, steps[0])
            own(dve.tensor_scalar(ang, ang, col("inv_freq"), None, ALU.mult))
            dve.wait_ge(dve_own_sem, steps[0])
            own(dve.tensor_scalar(tr1, ang, float(1.0 / (2 * np.pi)), 12582912.0, ALU.mult, ALU.add))
            dve.wait_ge(dve_own_sem, steps[0])
            own(dve.tensor_scalar(tr1, tr1, 12582912.0, None, ALU.subtract))
            two_pi = 2 * np.pi
            c1 = 6.28125
            c2 = float(np.float32(np.round((two_pi - c1) * 2 ** 21) / 2 ** 21))
            c3 = float(two_pi - c1 - c2)
            for cc in (c1, c2, c3):
                dve.wait_ge(dve_own_sem, steps[0])
                own(dve.scalar_tensor_tensor(out=ang, in0=tr1, scalar=-cc, in1=ang, op0=ALU.mult, op1=ALU.add))
            dve.wait_ge(dve_own_sem, steps[0])
            lim = 3.1415925
            own(dve.tensor_scalar(tr1, ang, lim, -lim, ALU.min, ALU.max))
            own(dve.tensor_scalar(ang, ang, float(np.pi / 2), None, ALU.add))
            dve.wait_ge(dve_own_sem, steps[0])
            own(dve.tensor_scalar(tr2, ang, float(np.pi), -two_pi, ALU.is_gt, ALU.mult))
            dve.wait_ge(dve_own_sem, steps[0])
            own(dve.tensor_tensor(tr2, tr2, ang, ALU.add))
            dve.wait_ge(dve_own_sem, steps[0])
            dve.tensor_scalar(tr2, tr2, lim, -lim, ALU.min, ALU.max).then_inc(fin_rope_sem, 1)
            next_rs()
            prepare(3, lambda t: gsc[:, t:t + 1], lambda t: mod[:, t:t + 1], hf, rsb[:, 0, :], hhi, hlo)
            dve.wait_ge(fin_rope_sem, 2)
            dve.wait_ge(dtab_in_sem, 16)

            def finish_c(h):
                next_rs()
                dve.wait_ge(o_split_sem, 8 + h)
                for b in range(2):
                    if b:
                        dve.wait_ge(dve_own_sem, steps[0])
                    own(dve.tensor_tensor(of[:, :, :], v2(ps[3 + b]), wide(rsb[:, 0, :], 2), ALU.mult))
                    dve.wait_ge(dve_own_sem, steps[0])
                    for t in range(2):
                        k = 2 * b + t
                        own(dve.scalar_tensor_tensor(out=of[:, t, :], in0=of[:, t, :], scalar=col("ret_gn", 4 * h + k), in1=zs_c[:, 4 * (h % 2) + k, :], op0=ALU.mult, op1=ALU.mult))
                    m = split_o(of[:, :, :], 4 * h + 2 * b, 2)
                    if b == 0:
                        own(m)
                m.then_inc(o_split_sem, 1)

            for h in range(4):
                J = JOB_C + 6 * h
                for k, to in enumerate((qn, kn)):
                    lows(J + k)
                    sums_done(J + k)
                    dve.wait_ge(sc_ok_sem, h)
                    dve.wait_ge(rope_ok_sem, 2 * h + k)
                    own(dve.tensor_tensor(rt1[:, :, :], bank(J + k), wide(cost, 2), ALU.mult))
                    dve.tensor_tensor(rt2[:, :, :], bank(J + k), wide(sint, 2), ALU.mult).then_inc(bank_free[(J + k) % 2], 1)
                    dve.wait_ge(dve_own_sem, steps[0])
                    dve.wait_ge(bank_free[(J + k) % 2], (J + k) // 2 + 1)
                    dve.tensor_tensor(to[:, 0, :], rt1[:, 0, :], rt2[:, 1, :], ALU.subtract)
                    dve.tensor_tensor(to[:, 1, :], rt2[:, 0, :], rt1[:, 1, :], ALU.add).then_inc(rope_ok_sem, 1)
                lows(J + 2)
                if h:
                    take_mod(2 + h)
                lows(J + 3)
                dve.wait_ge(sc_ok_sem, h + 1)
                dve.wait_ge(o_ok_sem, 8 + h)
                dve.tensor_tensor(sd, ps[5][:, 0:384], dmat[:, h, :], ALU.mult).then_inc(sd_ok_sem, 1)
                lows(J + 4)
                if h:
                    finish_c(h - 1)
                lows(J + 5)
            finish_c(3)
            take_mod(6)
            dve.wait_ge(mod_ok_sem, 7)
            add_x(JOB_OUT_C, gate=16)
            scaled_gain(1)
            dve.wait_ge(dve_own_sem, steps[0])
            next_rs()
            prepare(4, lambda t: gsc[:, 8 + t:9 + t], lambda t: mod[:, 24 + t:25 + t], hf, rsb[:, 0, :], hhi, hlo)
            dve.wait_ge(bias_ok_sem, 96)
            dve.wait_ge(boot_sem, 4)
            attend(JOB_D, 8, 4, A(bias_at, 16, 384), True, {5: 7})
            dve.wait_ge(mod_ok_sem, 8)
            add_x(JOB_OUT_D, gate=40)


def shape_tables():
    import math
    cst = np.zeros((P, N_CONST), np.float32)
    cst[:, C_IDENT:C_IDENT + P] = np.eye(P)
    j, i = np.arange(P)[:, None], np.arange(P)[None, :]
    cst[:, C_CAUSAL:C_CAUSAL + P] = np.where(i >= j, 0, NEG)
    cst[:, C_STRICT:C_STRICT + P] = np.where(i > j, -1, 0)
    n = np.arange(S)
    nf = np.maximum(n, 1).astype(np.float32)
    large = 16 + (np.log(nf / np.float32(16)) / np.float32(math.log(2048 / 16)) * np.float32(16)).astype(np.int32)
    bucket = np.where(n < 16, n, np.minimum(large, 31))
    for t in range(S):
        cst[bucket[S - 1 - t], C_ONEHOT + t] = 1
    lmask = np.zeros((P, LEVELS, 64), np.int32)
    for lv in range(LEVELS):
        w = 1 << lv
        left = [c for c in range(P) if (c // w) % 2 == 0]
        for k, c in enumerate(left):
            lmask[c // (2 * w) * 2 * w + w:c // (2 * w) * 2 * w + 2 * w, lv, k] = 1
    dtab = np.zeros((P, 4, 384), np.float32)
    lg = np.log(1.0 - 2.0 ** (-5.0 - np.arange(4, dtype=np.float64)))
    jj, ii = np.arange(S)[:, None], np.arange(S)[None, :]
    for h in range(4):
        full = np.where(jj // 64 <= ii // 64, np.exp(lg[h] * np.abs(ii - jj)), 0) / 16
        dtab[:, h, 0:256] = full[0:P]
        dtab[:, h, 256:384] = full[P:, P:]
    inv = (1.0 / (np.float32(10000.0) ** (np.arange(0, 256, 2, dtype=np.float32) / np.float32(256)))).astype(np.float32)
    return cst, lmask.reshape(P, LEVELS * 64), dtab, inv


def laid_out(z):
    def split(w, rows0, cols0):
        return w[rows0:rows0 + D, cols0:cols0 + 256].reshape(KT, P, 256).transpose(1, 0, 2).reshape(P, KT * 256)

    chunks = []
    w = z["a_w_in"][0]
    for i in range(4):
        for k in range(3):
            chunks.append(split(w, 0, 1024 * k + 256 * i))
    for i in range(4):
        chunks.append(split(w, 0, 3 * 1024 + 256 * i))
    for n in range(4):
        chunks.append(split(z["a_w_out"][0], 0, 256 * n))
    for i in range(4):
        chunks.append(split(z["b_w_in"][0], 0, 256 * i))
        chunks.append(split(z["w_kv"], 0, 256 * i))
        chunks.append(split(z["b_w_in"][0], 0, 1024 + 256 * i))
        chunks.append(split(z["w_kv"], 0, 1024 + 256 * i))
    for n in range(4):
        chunks.append(split(z["b_w_out"][0], 0, 256 * n))
    w = z["ret_w_in_2"][0]
    for h in range(4):
        for c0 in (256 * h, 1024 + 256 * h, 4096 + 512 * h, 4096 + 512 * h + 256, 2048 + 512 * h, 2048 + 512 * h + 256):
            chunks.append(split(w, 0, c0))
    for n in range(4):
        for hf in range(2):
            chunks.append(split(z["ret_w_out_2"][0], D * hf, 256 * n))
    w = z["att_w_in_2"][0]
    for i in range(8):
        for c0 in (0, 2048, 6144, 4096):
            chunks.append(split(w, 0, c0 + 256 * i))
    for n in range(4):
        for hf in range(2):
            chunks.append(split(z["att_w_out_2"][0], D * hf, 256 * n))
    ada = []
    for l in range(2):
        for u in range(24):
            ada.append(z["ada_w_2"][l][:, 128 * u:128 * u + 128].reshape(KT, P, 128).transpose(1, 0, 2).reshape(P, KT * 128))

    def down(v):
        return v.reshape(-1, P).T

    cst, lmask, dtab, inv = shape_tables()
    rows = np.zeros((P, 2), np.float32)
    rows[0:8, 0] = z["a_dt_bias"][0]
    rows[0:8, 1] = z["a_log"][0]
    conv = z["a_conv_w"][0].reshape(4, 24, P).transpose(2, 1, 0).reshape(P, 96)
    cols = np.concatenate([down(z["a_norm_g"][0]), down(z["kv_norm_g"]), down(z["b_norm_g"][0]), down(z["final_norm_g"]),
                           down(z["norm_g_2"].reshape(-1)), down(z["ret_gn_g_2"][0]), down(z["att_q_g_2"][0]),
                           down(z["att_k_g_2"][0]), down(z["a_out_norm_g"][0]), conv, down(z["c_2"][0]),
                           down(z["ada_b_2"].reshape(-1)), rows, inv[:, None]], axis=1)
    return {
        "x_t": z["x"][0].T.reshape(KT, P, S).transpose(1, 0, 2),
        "weights": np.stack(chunks),
        "ada": np.stack(ada),
        "cols": cols,
        "consts": cst,
        "join_masks": lmask,
        "w_ab": z["a_w_in"][0][:, 4096:4112].reshape(KT, P, 16).transpose(1, 0, 2),
        "rel_b": z["rel_bias"],
        "rel_d": z["att_rel_bias_2"][0][:, ::-1],
        "decay": dtab,
        "positions": z["positions_2"],
    }


def kernel(**inputs):
    import concourse.bacc as _bacc
    from concourse.bass_utils import run_bass_kernel_spmd as _run

    z = {k: np.asarray(v) for k, v in inputs.items()}
    arrays = {k: np.ascontiguousarray(v) for k, v in laid_out(z).items()}
    nc = _bacc.Bacc("TRN2", target_bir_lowering=False, num_devices=1)
    aps = [nc.dram_tensor(k, v.shape, mybir.dt.from_np(v.dtype), kind="ExternalInput").ap() for k, v in arrays.items()]
    out = nc.dram_tensor("out_t", (P, KT, S), F32, kind="ExternalOutput").ap()
    scr_b = nc.dram_tensor("bias_rows_b", (P, 8, 512), F32, kind="Internal").ap()
    scr_d = nc.dram_tensor("bias_rows_d", (P, 16, 512), F32, kind="Internal").ap()
    x_in, wts, ada_w, cols_in, const_in, lmask_in, w_ab, rel_b, rel_d, dtab, pos = aps
    two_blocks(nc, x_in, wts, ada_w, cols_in, const_in, lmask_in, w_ab, rel_b, rel_d, dtab, pos, out, scr_b, scr_d)
    r = _run(nc, [arrays], core_ids=[0])
    got = r.results[0]["out_t"]
    return np.ascontiguousarray(got.transpose(2, 1, 0).reshape(1, S, D))
```
